# Optimizing a Trainium2 kernel written in Bass

```python
import jax, jax.numpy as jnp
from jax import lax
import numpy as np

D_MODEL = 2048
BATCH = 1
SEQ = 256
DEPTH = 1

A_HEADS = 16
A_HEAD_DIM = 128
IDX_HEADS = 16
IDX_DIM = 64
INDEX_TOPK_MAX = 256
B_HEADS = 16
Q_LORA = 512
KV_LORA = 512
QK_NOPE = 128
QK_ROPE = 64
V_HEAD = 128
ROPE_THETA = 10000.0
D_FF = 5632
CONV_W = 3
PLE_DIM = 256
N_BRANCH = 2
Q_BLOCK = 128
DEEPNORM_ALPHA = (2.0 * DEPTH) ** 0.25
DEEPNORM_BETA = (8.0 * DEPTH) ** -0.25
LN_EPS = 1e-5
RMS_EPS = 1e-6
NEG = -1e30

SPLITS = (
    A_HEADS * A_HEAD_DIM,
    A_HEAD_DIM,
    A_HEAD_DIM,
    IDX_HEADS * IDX_DIM,
    IDX_DIM,
    IDX_HEADS,
    Q_LORA,
    KV_LORA,
    QK_ROPE,
    N_BRANCH * D_MODEL,
)
D_IN = sum(SPLITS)

kernel_name = "hybrid_dsa_mla_convffn_deepnorm_block"

def layer_norm(x, g, b):
    xf = x.astype(jnp.float32)
    mu = xf.mean(-1, keepdims=True)
    var = jnp.square(xf - mu).mean(-1, keepdims=True)
    return ((xf - mu) * lax.rsqrt(var + LN_EPS) * g + b).astype(x.dtype)

def rms_norm(x, g):
    xf = x.astype(jnp.float32)
    y = xf * lax.rsqrt(jnp.mean(xf * xf, -1, keepdims=True) + RMS_EPS)
    return (y * g).astype(x.dtype)

def rope_tables(S, dtype):
    pos = jnp.arange(S, dtype=jnp.float32)
    inv_freq = jnp.power(ROPE_THETA, -jnp.arange(0, QK_ROPE, 2, dtype=jnp.float32) / QK_ROPE)
    ang = pos[:, None] * inv_freq[None, :]
    return jnp.cos(ang).astype(dtype), jnp.sin(ang).astype(dtype)

def apply_rope(x, cos, sin):
    x1, x2 = jnp.split(x, 2, axis=-1)
    return jnp.concatenate([x1 * cos - x2 * sin, x1 * sin + x2 * cos], axis=-1)

def alibi_slopes(n_heads):
    return jnp.exp2(-8.0 * jnp.arange(1, n_heads + 1, dtype=jnp.float32) / n_heads)

def to_blocks(a, nb):
    return a.reshape(a.shape[0], nb, Q_BLOCK, *a.shape[2:]).swapaxes(0, 1)

def dsa_attention(q, k, v, q_idx, k_idx, w_idx, topk):
    B, S, H, Dh = q.shape
    nb = S // Q_BLOCK
    slopes = alibi_slopes(H)
    key_pos = jnp.arange(S)
    gather = jax.vmap(lambda a, i: a[i])
    scale = Dh ** -0.5

    def block(args):
        qb, qib, wib, blk = args
        t = blk * Q_BLOCK + jnp.arange(Q_BLOCK)
        s = jax.nn.relu(jnp.einsum('bqhd,bsd->bqhs', qib, k_idx))
        score = jnp.einsum('bqhs,bqh->bqs', s, wib).astype(jnp.float32)
        causal = key_pos[None, :] <= t[:, None]
        score = jnp.where(causal[None], score, NEG)
        _, idx = lax.top_k(score, topk)
        k_sel = gather(k, idx)
        v_sel = gather(v, idx)
        dist = (t[None, :, None] - idx).astype(jnp.float32)
        logits = jnp.einsum('bqhd,bqkd->bqhk', qb, k_sel).astype(jnp.float32) * scale
        logits = logits - slopes[:, None] * dist[:, :, None, :]
        logits = jnp.where((dist >= 0.0)[:, :, None, :], logits, NEG)
        probs = jax.nn.softmax(logits, axis=-1).astype(v.dtype)
        return jnp.einsum('bqhk,bqkd->bqhd', probs, v_sel)

    out = lax.map(block, (to_blocks(q, nb), to_blocks(q_idx, nb), to_blocks(w_idx, nb), jnp.arange(nb)))
    return out.swapaxes(0, 1).reshape(B, S, H * Dh)

def mla_attention(q_nope, q_pe, k_nope, k_pe, v):
    B, S, H, _ = q_nope.shape
    nb = S // Q_BLOCK
    key_pos = jnp.arange(S)
    scale = (QK_NOPE + QK_ROPE) ** -0.5

    def block(args):
        qn, qr, blk = args
        t = blk * Q_BLOCK + jnp.arange(Q_BLOCK)
        logits = (jnp.einsum('bqhd,bshd->bhqs', qn, k_nope)
                  + jnp.einsum('bqhr,bsr->bhqs', qr, k_pe)).astype(jnp.float32) * scale
        causal = key_pos[None, :] <= t[:, None]
        logits = jnp.where(causal[None, None], logits, NEG)
        probs = jax.nn.softmax(logits, axis=-1).astype(v.dtype)
        return jnp.einsum('bhqs,bshd->bqhd', probs, v)

    out = lax.map(block, (to_blocks(q_nope, nb), to_blocks(q_pe, nb), jnp.arange(nb)))
    return out.swapaxes(0, 1).reshape(B, S, H * V_HEAD)

def causal_dwconv(u, w, b):
    S = u.shape[1]
    up = jnp.pad(u, ((0, 0), (CONV_W - 1, 0), (0, 0)))
    y = up[:, 0:S] * w[0]
    for j in range(1, CONV_W):
        y = y + up[:, j:j + S] * w[j]
    return y + b

def setup_inputs(seed: int = 0) -> dict:
    key = jax.random.key(seed)
    ks = jax.random.split(key, 24)
    f32 = jnp.float32
    nrm = lambda k, shape, fan_in, gain=1.0: jax.random.normal(k, shape, f32) * (gain * fan_in ** -0.5)
    L = DEPTH
    return {
        'x': jax.random.normal(ks[0], (BATCH, SEQ, D_MODEL), f32),
        'p': jax.random.normal(ks[1], (DEPTH, BATCH, SEQ, PLE_DIM), f32),
        'w_in': nrm(ks[2], (L, D_MODEL, D_IN), D_MODEL),
        'q_a_norm': 1.0 + 0.02 * jax.random.normal(ks[3], (L, Q_LORA), f32),
        'kv_a_norm': 1.0 + 0.02 * jax.random.normal(ks[4], (L, KV_LORA), f32),
        'w_uq': nrm(ks[5], (L, Q_LORA, B_HEADS, QK_NOPE + QK_ROPE), Q_LORA),
        'w_uk': nrm(ks[6], (L, KV_LORA, B_HEADS, QK_NOPE), KV_LORA),
        'w_uv': nrm(ks[7], (L, KV_LORA, B_HEADS, V_HEAD), KV_LORA),
        'w_branch_a': nrm(ks[8], (L, A_HEADS * A_HEAD_DIM, D_MODEL), A_HEADS * A_HEAD_DIM),
        'w_branch_b': nrm(ks[9], (L, B_HEADS * V_HEAD, D_MODEL), B_HEADS * V_HEAD),
        'w_o': nrm(ks[10], (L, D_MODEL, D_MODEL), D_MODEL, DEEPNORM_BETA),
        'ln1_g': 1.0 + 0.02 * jax.random.normal(ks[11], (L, D_MODEL), f32),
        'ln1_b': 0.02 * jax.random.normal(ks[12], (L, D_MODEL), f32),
        'w_up': nrm(ks[13], (L, D_MODEL, 2 * D_FF), D_MODEL),
        'conv_w': nrm(ks[14], (L, CONV_W, 2 * D_FF), CONV_W),
        'conv_b': 0.02 * jax.random.normal(ks[15], (L, 2 * D_FF), f32),
        'w_down': nrm(ks[16], (L, D_FF, D_MODEL), D_FF, DEEPNORM_BETA),
        'w_pg': nrm(ks[17], (L, D_MODEL, D_MODEL), D_MODEL),
        'b_pg': 0.02 * jax.random.normal(ks[18], (L, D_MODEL), f32),
        'w_pe': nrm(ks[19], (L, PLE_DIM, D_MODEL), PLE_DIM),
        'ln2_g': 1.0 + 0.02 * jax.random.normal(ks[20], (L, D_MODEL), f32),
        'ln2_b': 0.02 * jax.random.normal(ks[21], (L, D_MODEL), f32),
    }

def reference(x, p, w_in, q_a_norm, kv_a_norm, w_uq, w_uk, w_uv, w_branch_a, w_branch_b, w_o,
              ln1_g, ln1_b, w_up, conv_w, conv_b, w_down, w_pg, b_pg, w_pe, ln2_g, ln2_b):
    B, S, _ = x.shape
    topk = min(INDEX_TOPK_MAX, S // 4)
    cos, sin = rope_tables(S, x.dtype)
    split_points = np.cumsum(SPLITS)[:-1].tolist()
    for i in range(DEPTH):
        u = x @ w_in[i]
        (q_a, k_a, v_a, q_idx, k_idx, w_idx, c_q, c_kv, k_pe, gate_logits) = jnp.split(u, split_points, axis=-1)
        attn_a = dsa_attention(q_a.reshape(B, S, A_HEADS, A_HEAD_DIM), k_a, v_a,
                               q_idx.reshape(B, S, IDX_HEADS, IDX_DIM), k_idx, w_idx, topk)
        c_q = rms_norm(c_q, q_a_norm[i])
        q_b = jnp.einsum('bsc,chd->bshd', c_q, w_uq[i])
        q_nope, q_pe = q_b[..., :QK_NOPE], q_b[..., QK_NOPE:]
        q_pe = apply_rope(q_pe, cos[:, None, :], sin[:, None, :])
        k_pe = apply_rope(k_pe, cos, sin)
        c_kv = rms_norm(c_kv, kv_a_norm[i])
        k_nope = jnp.einsum('bsc,chd->bshd', c_kv, w_uk[i])
        v_b = jnp.einsum('bsc,chd->bshd', c_kv, w_uv[i])
        attn_b = mla_attention(q_nope, q_pe, k_nope, k_pe, v_b)
        gates = jax.nn.sigmoid(gate_logits.reshape(B, S, N_BRANCH, D_MODEL))
        merged = gates[:, :, 0] * (attn_a @ w_branch_a[i]) + gates[:, :, 1] * (attn_b @ w_branch_b[i])
        x = layer_norm(DEEPNORM_ALPHA * x + merged @ w_o[i], ln1_g[i], ln1_b[i])
        hid = causal_dwconv(x @ w_up[i], conv_w[i], conv_b[i])
        h_gate, h_val = hid[..., :D_FF], hid[..., D_FF:]
        ffn = (jax.nn.silu(h_gate) * h_val) @ w_down[i]
        ple = jax.nn.sigmoid(x @ w_pg[i] + b_pg[i]) * (p[i] @ w_pe[i])
        x = layer_norm(DEEPNORM_ALPHA * x + ffn + ple, ln2_g[i], ln2_b[i])
    return x


_drawn_inputs = setup_inputs


def setup_inputs(seed=0):
    import zlib

    import numpy as np

    out = dict(_drawn_inputs(seed))
    spreads = {}
    factors = {'q_a_norm': 8.0,
     'kv_a_norm': 8.0,
     'ln1_g': 3.007,
     'ln1_b': 2.985,
     'conv_b': 7.559,
     'b_pg': 64.0,
     'ln2_g': 8.28,
     'ln2_b': 7.958}
    for name, (base, spread) in spreads.items():
        noise = np.random.default_rng([zlib.crc32(name.encode()), seed]).standard_normal(out[name].shape)
        drawn = base * np.exp(spread * noise) if base else spread * noise
        out[name] = __import__('jax').numpy.asarray(drawn.astype(out[name].dtype))
    for name, factor in factors.items():
        out[name] = (out[name] * factor).astype(out[name].dtype)
    return out
```

```python
from contextlib import ExitStack

import numpy as np

import concourse.bass as bass
from concourse import mybir

F32 = mybir.dt.float32
F32R = mybir.dt.float32r
ALU = mybir.AluOpType
ACT = mybir.ActivationFunctionType
AX_X = mybir.AxisListType.X

P = 128
S = 256
D = 2048
HEADS = 16
HD = 128
ROPE = 64
LORA = 512
TOPK = 64
FF = 5632
PLE = 256
ALPHA = 2.0 ** 0.25
LN_EPS = 1e-5
RMS_EPS = 1e-6
NEG = -1e30
SCALE_A = HD ** -0.5
SCALE_B = (HD + ROPE) ** -0.5

RING = 4
AHEAD = 3
BLK = 8
UNIT = BLK * P
DT = D // P
FT = FF // P
LT = LORA // P
N_FEAT = 20
T_KIDX, T_WIDX, T_KA, T_VA, T_QIDX, T_CQ, T_CKV = 0, 1, 2, 3, 4, 12, 16
SC = P + S
BLOCKS = ((0, 0, P), (1, P, S))

U_FEAT, U_QA, U_UQ, U_UK, U_UV = 2 * N_FEAT, 2 * DT, 12, 8, 8
U_GATE, U_BRANCH, U_PLE, U_O, U_PG, U_UP = 4 * DT, 4 * DT, 4, 2 * DT, 2 * DT, 4 * FT
U_DOWN_TILE = -(-FT // BLK)
DOWN_LAST = FT - (U_DOWN_TILE - 1) * BLK
U_BEFORE_DOWN = U_FEAT + U_QA + U_UQ + U_UK + U_UV + U_GATE + U_BRANCH + U_PLE + U_O + U_PG + U_UP
U_ALL = U_BEFORE_DOWN + U_DOWN_TILE * DT

C_CONV = 0
C_SLOPE = C_CONV + 8 * FT
C_LN1G = C_SLOPE + HEADS
C_LN1B = C_LN1G + DT
C_LN2G = C_LN1B + DT
C_LN2B = C_LN2G + DT
C_BPG = C_LN2B + DT
C_QN = C_BPG + DT
C_KVN = C_QN + LT
C_EPS = C_KVN + LT
N_PAR = C_EPS + 3

K_IDENT, K_ONES = 0, P
K_STAY = 2 * P
K_COS, K_SIN, K_ROT, K_DUP, K_DUPROT = 0, S, 2 * S, 2 * S + P, 2 * S + 2 * P
K_EARLY = 2 * S + 3 * P


class Count:

    def __init__(self, start=0):
        self.base, self.k = start, 0

    @property
    def value(self):
        return self.base + self.k

    def add(self, n=1):
        self.k += n


def repeat(eng, times, body, *counts):
    starts = [c.value for c, _ in counts]
    with eng.Fori(0, times) as i:
        for (c, n), s in zip(counts, starts):
            c.base, c.k = i * n + s, 0
        body(i)
        assert all(c.k == n for c, n in counts), [(c.k, n) for c, n in counts]
    for (c, n), s in zip(counts, starts):
        c.base, c.k = s + times * n, 0


def hybrid_block(nc, stream, x_t, p_t, params, consts_stay, consts_early, masks, out):
    with ExitStack() as ctx:
        def sb(name, shape, dt=F32):
            return ctx.enter_context(nc.sbuf_tensor(name, shape, dt))

        def overlay(*items):
            with ExitStack() as phase:
                return [phase.enter_context(nc.sbuf_tensor(n, s, d)) for n, s, d in items]

        def gap(name, kib):
            return (name, [P, kib * 256], F32)

        raw = sb("raw", [P, RING, UNIT])
        w_hi = sb("w_hi", [P, RING, UNIT], F32R)
        w_lo = sb("w_lo", [P, RING, UNIT], F32R)
        par = sb("par", [P, N_PAR])
        kc = sb("kc", [P, K_STAY])
        half = sb("half", [P, 2, S])
        tmp = sb("tmp", [P, 2, S])
        ident = kc[:, K_IDENT:K_IDENT + P]
        ones = kc[:, K_ONES:K_ONES + P]

        madd, dist, caus, ke, score, work, rel, qi_st, top8, cnt, spare = overlay(
            ("madd", [P, SC], F32), ("dist", [P, SC], F32), ("caus", [P, SC], F32),
            ("ke", [P, K_EARLY], F32), ("score", [P, SC], F32), ("work", [P, SC], F32),
            ("rel", [P, 2, SC], F32), ("qi_st", [P, S], F32), ("top8", [P, 2, 8], F32),
            ("cnt", [P, 2], F32), ("spare", [P, 1], F32))
        _, bias, prob, prob_t, qa_st, qn_st, qp_st, v_st, mx, nmx, sm, rsm = overlay(
            ("masks_", [P, 3 * SC], F32), ("bias", [P, SC], F32), ("prob", [P, 2, SC], F32),
            ("prob_t", [P, 2, SC], F32), ("qa_st", [P, S], F32), ("qn_st", [P, S], F32),
            ("qp_st", [P, S], F32), ("v_st", [P, 2, HD], F32), ("mx", [P, 4], F32),
            ("nmx", [P, 4], F32), ("sm", [P, 4], F32), ("rsm", [P, 4], F32))
        p_raw, p_hl, sq, mean, rowsum = overlay(
            ("p_raw", [P, 2, S], F32), ("p_hl", [P, 2, 2 * S], F32R), ("sq", [P, 2, 4 * S], F32),
            ("mean", [P, S], F32), ("rowsum", [P, S], F32))
        merged = sq[:, 0, 0:S]
        rstd = sq[:, 0, 0:S]
        sb("scratch", [P, 16 * 256 + 128])

        x_hl, qa, qk, v_mla, ka_s, kpe, va, wix, _, feat, c_hl = overlay(
            ("x_hl", [P, DT, 2 * S], F32R), ("qa", [P, DT, S], F32),
            ("qk", [P, 40, S], F32), ("v_mla", [P, 2, D], F32),
            ("ka_s", [P, S], F32), ("kpe", [P, S], F32), ("va", [P, 2, HD], F32),
            ("wix", [P, 2, HEADS], F32), gap("g1", 2),
            ("feat", [P, N_FEAT, S], F32), ("c_hl", [P, 2 * LT, 2 * S], F32R))
        qp, qn, kn = (qk[:, a:b] for a, b in ((0, 8), (8, 24), (24, 40)))
        _, x_raw = overlay(gap("g2", 88), ("x_raw", [P, DT, S], F32))
        _, c_sq, c_std = overlay(gap("g2b", 88), ("c_sq", [P, 2, LT, S], F32), ("c_std", [P, 2, S], F32))
        oa_hl, m_hl, _, ob_hl, _, gate = overlay(
            ("oa_hl", [P, DT, 2 * S], F32R), ("m_hl", [P, DT, 2 * S], F32R), gap("g3", 8),
            ("ob_hl", [P, DT, 2 * S], F32R), gap("g4", 5), ("gate", [P, 2 * DT, S], F32))
        res, _, ple = overlay(("res", [P, DT, S], F32), gap("g5", 95), ("ple", [P, DT, S], F32))
        _, x1_hl = overlay(gap("g6", 16), ("x1_hl", [P, DT, 2 * S], F32R))
        _, act_hl, u, cv, th, av = overlay(
            gap("g7", 48), ("act_hl", [P, FT, 2 * S], F32R), ("u", [P, 2, S + 2], F32),
            ("cv", [P, 2, S], F32), ("th", [P, S], F32), ("av", [P, S], F32))

        bank = [ctx.enter_context(nc.psum_tensor(f"bank{i}", [P, 2 * S], F32)) for i in range(8)]

        def sem(name):
            return ctx.enter_context(nc.semaphore(name))

        loaded = [sem(f"loaded{s}") for s in range(RING)]
        hi_done = sem("hi_done")
        lo_done = sem("lo_done")
        mm_done = sem("mm_done")
        half_done = sem("half_done")
        bank_free = sem("bank_free")
        par_in, kc_in, ke_in, caus_in, dist_in, p_in, res_in = (sem(n) for n in (
            "par_in", "kc_in", "ke_in", "caus_in", "dist_in", "p_in", "res_in"))
        x_in = [sem(f"x_in{c}") for c in range(4)]
        x_hi, x_lo = sem("x_hi"), sem("x_lo")
        pre_mm, pre_read = sem("pre_mm"), sem("pre_read")
        qi_staged, idx_mm, relu_done, idx_used = (sem(n) for n in (
            "qi_staged", "idx_mm", "relu_done", "idx_used"))
        rms_sq, rms_mm, rms_std, rms_n, rms_hi, rms_lo = (sem(n) for n in (
            "rms_sq", "rms_mm", "rms_std", "rms_n", "rms_hi", "rms_lo"))
        rot_mm, rot_done = sem("rot_mm"), sem("rot_done")
        topk_done = sem("topk_done")
        q_staged, v_staged, sc_a, sc_b, nmx_ready, exp_done, prob_ready = (sem(n) for n in (
            "q_staged", "v_staged", "sc_a", "sc_b", "nmx_ready", "exp_done", "prob_ready"))
        tr_mm, pt_a, pt_b, pv_mm, o_out, gate_th = (sem(n) for n in (
            "tr_mm", "pt_a", "pt_b", "pv_mm", "o_out", "gate_th"))
        o_hi, o_lo, m_lo, p_hi, p_lo = (sem(n) for n in ("o_hi", "o_lo", "m_lo", "p_hi", "p_lo"))
        row_added, ln_mm, ln_mean, ln_cen, ln_sq, ln_sqmm, ln_std, ln_n, ln_aff, x1_lo = (
            sem(n) for n in ("row_added", "ln_mm", "ln_mean", "ln_cen", "ln_sq", "ln_sqmm", "ln_std",
                             "ln_n", "ln_aff", "x1_lo"))
        pg_sum, pg_th, cv_done, th_done, act_lo = (sem(n) for n in (
            "pg_sum", "pg_th", "cv_done", "th_done", "act_lo"))
        dve_step = sem("dve_step")
        out_done = sem("out_done")

        block = ctx.enter_context(nc.Block())

        @block.sync
        def _(sp):
            for c in range(4):
                sp.dma_start(x_raw[:, 4 * c:4 * c + 4], x_t[:, 4 * c:4 * c + 4]).then_inc(x_in[c], 16)
                sp.dma_start(raw[:, c], stream[c]).then_inc(loaded[c], 16)
            sp.dma_start(par[:], params).then_inc(par_in, 16)
            sp.dma_start(kc[:], consts_stay).then_inc(kc_in, 16)
            sp.dma_start(ke[:], consts_early).then_inc(ke_in, 16)
            sp.dma_start(caus[:], masks[0]).then_inc(caus_in, 16)
            sp.dma_start(dist[:], masks[1]).then_inc(dist_in, 16)

            def load_four(i):
                for s in range(RING):
                    sp.wait_ge(lo_done, i * RING + (s - RING + 1))
                    sp.dma_start(raw[:, s], stream[i * RING + s]).then_inc(loaded[s], 16)

            behind = U_FEAT + U_QA + U_UQ + U_UK + U_UV + U_GATE + U_BRANCH
            with sp.Fori(1, behind // RING) as i:
                load_four(i)
            sp.wait_ge(pv_mm, HEADS + 1)
            sp.wait_ge(o_out, HEADS + 2)
            sp.dma_start(p_raw[:], p_t).then_inc(p_in, 16)
            load_four(behind // RING)
            sp.wait_ge(mm_done, behind + 1)
            sp.dma_start(res[:], x_t).then_inc(res_in, 16)
            with sp.Fori(behind // RING + 1, U_BEFORE_DOWN // RING) as i:
                load_four(i)

            with sp.Fori(0, DT // 2) as i:
                for s in range(2 * U_DOWN_TILE):
                    n = (DOWN_LAST if s % U_DOWN_TILE == U_DOWN_TILE - 1 else BLK) * P
                    sp.wait_ge(lo_done, i * (2 * U_DOWN_TILE) + (U_BEFORE_DOWN + s - RING + 1))
                    sp.dma_start(raw[:, s % RING, 0:n],
                                 stream[i * (2 * U_DOWN_TILE) + (U_BEFORE_DOWN + s), :, 0:n]
                                 ).then_inc(loaded[s % RING], 16)

            for c in range(4):
                sp.wait_ge(ln_aff, DT + 4 * (c + 1))
                sp.dma_start(out[:, 4 * c:4 * c + 4], res[:, 4 * c:4 * c + 4]).then_inc(out_done, 16)
            sp.wait_ge(out_done, 4 * 16)

        @block.tensor
        def _(pe):
            U, T = Count(), Count()
            pe.sem_inc(mm_done, 1)
            pe.sem_inc(idx_mm, 1)
            pe.sem_inc(sc_b, 1)
            pe.sem_inc(pv_mm, 1)

            def block_mm(s, c, b, x, first, last):
                w = slice(c * P, c * P + P)
                pe.matmul(bank[b][:], w_hi[:, s, w], x, start=first, stop=False)
                return pe.matmul(bank[b][:, S:2 * S], w_lo[:, s, w], x[:, 0:S], start=False, stop=last)

            def take_unit():
                pe.wait_ge(lo_done, U.value + 1)

            def take_bank(users=2):
                pe.wait_ge(bank_free, T.value + (3 - users))

            def unit_of_tile(s, b, x, k0, n=BLK, first=False, last=False):
                take_unit()
                if first:
                    take_bank()
                for c in range(n):
                    ins = block_mm(s, c, b, x[:, k0 + c], first and c == 0, last and c == n - 1)
                ins.then_inc(mm_done, 1)
                U.add()
                if last:
                    T.add()

            def two_tiles(xs, before=None):
                def body(i):
                    if before:
                        before(i)
                    for s in range(4):
                        unit_of_tile(s, s // 2, xs[s // 2], BLK * (s % 2), first=s % 2 == 0, last=s % 2 == 1)
                return body

            STD = ((U, 4), (T, 2))
            x2 = (x_hl, x_hl)

            def tiles_of_unit(x, k0, nk, per):
                def body(i):
                    for s in range(4):
                        take_unit()
                        for t in range(per):
                            b = (s * per + t) % 4
                            take_bank(4)
                            for k in range(nk):
                                ins = block_mm(s, t * nk + k, b, x[:, k0 + k], k == 0, k == nk - 1)
                            T.add()
                        ins.then_inc(mm_done, 1)
                        U.add()
                return body

            pe.wait_ge(x_lo, 2)
            unit_of_tile(0, 0, x_hl, 0, first=True)
            pe.wait_ge(x_lo, 4)
            unit_of_tile(1, 0, x_hl, BLK, last=True)
            unit_of_tile(2, 1, x_hl, 0, first=True)
            unit_of_tile(3, 1, x_hl, BLK, last=True)
            repeat(pe, N_FEAT // 2 - 1, two_tiles(x2), *STD)

            pe.wait_ge(kc_in, 16)
            pe.wait_ge(ke_in, 16)
            pe.wait_ge(bank_free, 2 + 4)
            for n, t in enumerate((T_WIDX, T_VA)):
                for tb in range(2):
                    pe.transpose(bank[6][:, (2 * n + tb) * P:(2 * n + tb + 1) * P],
                                 feat[:, t, tb * P:tb * P + P], ident)
            pe.matmul(bank[7][:, 0:S], ke[:, K_DUP:K_DUP + P], feat[:, T_KIDX], start=True, stop=True)
            pe.matmul(bank[7][:, S:2 * S], ke[:, K_DUPROT:K_DUPROT + P], feat[:, T_KIDX],
                      start=True, stop=True).then_inc(pre_mm, 1)

            J = Count()

            def indexer(i):
                pe.wait_ge(qi_staged, J.value + 1)
                pe.wait_ge(relu_done, 2 * J.value + 2)
                for b in range(2):
                    h = slice(ROPE * b, ROPE * b + ROPE)
                    key = feat[h, T_KIDX if b == 0 else T_WIDX]
                    for q, c0, nk in BLOCKS:
                        ins = pe.matmul(bank[4 + b][:, c0:c0 + nk], qi_st[h, q * P:q * P + P],
                                        key[:, 0:nk], start=True, stop=True)
                ins.then_inc(idx_mm, 1)
                J.add()

            pe.wait_ge(bank_free, 2 + 12)
            repeat(pe, 4, two_tiles(x2, indexer), *STD, (J, 1))
            pe.wait_ge(pre_read, 1)
            for n in range(2):
                pe.wait_ge(rms_sq, n + 1)
                for t in range(LT):
                    ins = pe.matmul(bank[6 + n][:, 0:S], ones, c_sq[:, n, t], start=t == 0, stop=t == LT - 1)
                ins.then_inc(rms_mm, 1)
            repeat(pe, 4, two_tiles(x2, indexer), *STD, (J, 1))

            pe.wait_ge(bank_free, T.value + 2)
            pe.wait_ge(rms_lo, 1)
            repeat(pe, U_UQ // 4, tiles_of_unit(c_hl, 0, LT, 2), (U, 4), (T, 8))
            pe.wait_ge(rms_lo, 2)
            repeat(pe, U_UK // 4, tiles_of_unit(c_hl, LT, LT, 2), (U, 4), (T, 8))

            def values_and_rope(i):
                for s in range(4):
                    take_unit()
                    take_bank()
                    for tb in range(2):
                        o = bank[s % 2][:, tb * S:tb * S + S]
                        for k in range(LT):
                            c_hi = c_hl[:, LT + k, tb * P:tb * P + P]
                            c_lo = c_hl[:, LT + k, S + tb * P:S + tb * P + P]
                            w = slice(k * S, k * S + S)
                            pe.matmul(o, c_hi, w_hi[:, s, w], start=k == 0, stop=False)
                            pe.matmul(o, c_hi, w_lo[:, s, w], start=False, stop=False)
                            ins = pe.matmul(o, c_lo, w_hi[:, s, w], start=False, stop=k == LT - 1)
                    ins.then_inc(mm_done, 1)
                    U.add()
                    T.add()
                    pe.wait_ge(rot_done, J.value + 1)
                    pe.matmul(bank[4 + s % 2][:, 0:S], ke[:, K_ROT:K_ROT + P],
                              qp[:, i * 4 + s], start=True, stop=True).then_inc(rot_mm, 1)
                    J.add()

            J = Count()
            pe.wait_ge(bank_free, T.value + 2)
            repeat(pe, U_UV // 4, values_and_rope, (U, 4), (T, 4), (J, 4))

            Hd = Count()

            def heads(i):
                for par_ in range(2):
                    half_ = slice(ROPE * par_, ROPE * par_ + ROPE)
                    h = Hd.value
                    pe.wait_ge(q_staged, h + 1)
                    for q, c0, nk in BLOCKS:
                        ins = pe.matmul(bank[2][:, c0:c0 + nk], qa_st[:, q * P:q * P + P], ka_s[:, 0:nk],
                                        start=True, stop=True)
                    ins.then_inc(sc_a, 1)
                    for q, c0, nk in BLOCKS:
                        pe.matmul(bank[3][:, c0:c0 + nk], qn_st[:, q * P:q * P + P],
                                  kn[:, i * 2 + par_, 0:nk], start=True, stop=False)
                        ins = pe.matmul(bank[3][:, c0:c0 + nk], qp_st[half_, q * P:q * P + P],
                                        kpe[half_, 0:nk], start=False, stop=True)
                    ins.then_inc(sc_b, 1)
                    unit_of_tile(0, 0, x_hl, 0, first=True)
                    unit_of_tile(1, 0, x_hl, BLK, last=True)
                    pe.wait_ge(prob_ready, 4 * h + 4)
                    for m in range(2):
                        for c in range(3):
                            ins = pe.transpose(bank[4 + m][:, c * P:c * P + P], prob[:, m, c * P:c * P + P], ident)
                    ins.then_inc(tr_mm, 1)
                    unit_of_tile(2, 1, x_hl, 0, first=True)
                    pe.wait_ge(pt_a, h + 1)
                    pe.wait_ge(pt_b, h + 1)
                    pe.wait_ge(v_staged, h + 1)
                    pe.wait_ge(o_out, h + 1)
                    for m, v in enumerate((va, v_st)):
                        pe.matmul(bank[6 + par_][:, m * S:m * S + S], v[:, 0], prob_t[:, m, 0:S],
                                  start=True, stop=False)
                        ins = pe.matmul(bank[6 + par_][:, m * S + P:m * S + S], v[:, 1], prob_t[:, m, S:SC],
                                        start=False, stop=True)
                    ins.then_inc(pv_mm, 1)
                    unit_of_tile(3, 1, x_hl, BLK, last=True)
                    Hd.add()

            pe.wait_ge(pre_read, 2)
            repeat(pe, HEADS // 2, heads, (U, 8), (T, 4), (Hd, 2))

            pe.wait_ge(o_lo, 8)
            repeat(pe, DT, two_tiles((oa_hl, ob_hl)), *STD)

            pe.wait_ge(bank_free, T.value + 2)
            pe.wait_ge(p_lo, 1)
            tiles_of_unit(p_hl, 0, 2, 4)(0)

            def norm_sums(w):
                pe.wait_ge(row_added, DT * (w + 1) + 1)
                pe.matmul(bank[6][:, 0:S], ones, rowsum[:], start=True, stop=True).then_inc(ln_mm, 1)
                for c in range(4):
                    pe.wait_ge(ln_sq, 4 * w + c + 1)
                    for t in range(4):
                        ins = pe.matmul(bank[7][:, 0:S], ones, sq[:, c % 2, t * S:t * S + S],
                                        start=c + t == 0, stop=c == 3 and t == 3)
                    ins.then_inc(ln_sqmm, 1)

            pe.wait_ge(m_lo, DT)
            repeat(pe, DT // 2, two_tiles((m_hl, m_hl)), *STD)
            norm_sums(0)

            pe.wait_ge(x1_lo, 4)
            repeat(pe, DT // 2, two_tiles((x1_hl, x1_hl)), *STD)
            repeat(pe, FT, two_tiles((x1_hl, x1_hl)), *STD)

            def down(i):
                for s in range(2 * U_DOWN_TILE):
                    t, c = divmod(s, U_DOWN_TILE)
                    lastu = c == U_DOWN_TILE - 1
                    unit_of_tile(s % RING, t, act_hl, c * BLK, DOWN_LAST if lastu else BLK,
                                 first=c == 0, last=lastu)

            pe.wait_ge(act_lo, FT)
            repeat(pe, DT // 2, down, (U, 2 * U_DOWN_TILE), (T, 2))
            norm_sums(1)

        @block.scalar
        def _(act):
            U, T = Count(), Count()
            act.sem_inc(relu_done, 2)
            act.sem_inc(gate_th, 2)

            def split_hi(s, n=UNIT):
                v, turn = (s + AHEAD) % RING, (s + AHEAD) // RING
                act.wait_ge(loaded[v], (U.value - s) * (16 // RING) + 16 * (turn + 1))
                act.wait_ge(mm_done, U.value + 1)
                act.activation(w_hi[:, v, 0:n], raw[:, v, 0:n], ACT.Copy).then_inc(hi_done, 1)

            def read_half(b, scale=1.0):
                act.wait_ge(mm_done, U.value + 1)
                act.wait_ge(bank_free, T.value + 1)
                act.activation(half[:, b % 2], bank[b][:, 0:S], ACT.Copy, scale=scale).then_inc(half_done, 1)
                T.add()

            def two_tiles(scale=1.0, after=None):
                def body(i):
                    for s in range(4):
                        split_hi(s)
                        U.add()
                        if s % 2:
                            read_half(s // 2, scale)
                            if after:
                                after(i, s // 2)
                return body

            def tiles_of_unit(per):
                def body(i):
                    for s in range(4):
                        split_hi(s)
                        U.add()
                        for t in range(per):
                            read_half((s * per + t) % 4)
                return body

            STD = ((U, 4), (T, 2))

            for c in range(4):
                act.wait_ge(x_in[c], 16)
                act.activation(x_hl[:, 4 * c:4 * c + 4, 0:S], x_raw[:, 4 * c:4 * c + 4], ACT.Copy
                               ).then_inc(x_hi, 1)
                if c < AHEAD:
                    act.wait_ge(loaded[c], 16)
                    act.activation(w_hi[:, c], raw[:, c], ACT.Copy).then_inc(hi_done, 1)

            repeat(act, N_FEAT // 2, two_tiles(), *STD)
            for n, t in enumerate((T_CQ, T_CKV)):
                act.wait_ge(bank_free, 2 + N_FEAT)
                act.activation(c_sq[:, n], feat[:, t:t + LT], ACT.Square).then_inc(rms_sq, 1)

            J = Count()

            def indexer(i, b):
                if b == 0:
                    return
                act.wait_ge(idx_mm, J.value + 2)
                for b in range(2):
                    act.wait_ge(idx_used, 2 * J.value + 1 + b)
                    act.activation(rel[:, b], bank[4 + b][:, 0:SC], ACT.Relu).then_inc(relu_done, 1)
                J.add()

            repeat(act, 4, two_tiles(after=indexer), *STD, (J, 1))
            act.wait_ge(par_in, 16)
            for n in range(2):
                act.wait_ge(rms_mm, n + 1)
                k = SCALE_B ** 2 if n == 0 else 1.0
                e = C_EPS + (2 if n == 0 else 1)
                act.activation(c_std[:, n], bank[6 + n][:, 0:S], ACT.Sqrt, scale=1.0 / (LORA * k),
                               bias=par[:, e:e + 1]).then_inc(rms_std, 1)
            for n, t in enumerate((T_CQ, T_CKV)):
                act.wait_ge(rms_n, LT * (n + 1))
                act.activation(c_hl[:, LT * n:LT * n + LT, 0:S], feat[:, t:t + LT], ACT.Copy
                               ).then_inc(rms_hi, 1)
            repeat(act, 4, two_tiles(after=indexer), *STD, (J, 1))

            repeat(act, (U_UQ + U_UK) // 4, tiles_of_unit(2), (U, 4), (T, 8))

            def values(i):
                for s in range(4):
                    split_hi(s)
                    U.add()
                    T.add()

            repeat(act, U_UV // 4, values, (U, 4), (T, 4))

            Hd = Count()

            def heads(i):
                for par_ in range(2):
                    h = Hd.value
                    split_hi(0)
                    U.add()
                    act.wait_ge(nmx_ready, h + 1)
                    for m in range(2):
                        for q, c0, nk in BLOCKS:
                            c = 2 * m + q
                            act.activation(prob[:, m, c0:c0 + nk], prob[:, m, c0:c0 + nk], ACT.Exp,
                                           bias=nmx[:, c:c + 1], accum_out=sm[:, c:c + 1]).then_inc(exp_done, 1)
                    split_hi(1)
                    U.add()
                    read_half(0)
                    split_hi(2)
                    U.add()
                    act.wait_ge(bank_free, T.value + 2)
                    act.activation(gate[:, i * 4 + 2 * par_], tmp[:, 0], ACT.Tanh, scale=0.5).then_inc(gate_th, 1)
                    act.wait_ge(tr_mm, h + 1)
                    act.wait_ge(pv_mm, h + 1)
                    act.activation(prob_t[:, 0], bank[4][:, 0:SC], ACT.Copy).then_inc(pt_a, 1)
                    split_hi(3)
                    U.add()
                    read_half(1)
                    act.wait_ge(bank_free, T.value + 2)
                    act.activation(gate[:, i * 4 + 2 * par_ + 1], tmp[:, 1], ACT.Tanh, scale=0.5
                                   ).then_inc(gate_th, 1)
                    Hd.add()

            repeat(act, HEADS // 2, heads, (U, 8), (T, 4), (Hd, 2))

            act.wait_ge(mm_done, U.value + 1)
            act.wait_ge(o_out, HEADS + 2)
            for src, dst in ((qa, oa_hl), (qn, ob_hl)):
                for c in range(4):
                    act.activation(dst[:, 4 * c:4 * c + 4, 0:S], src[:, 4 * c:4 * c + 4], ACT.Copy
                                   ).then_inc(o_hi, 1)
            repeat(act, DT, two_tiles(0.5), *STD)

            act.wait_ge(p_in, 16)
            act.activation(p_hl[:, :, 0:S], p_raw[:], ACT.Copy).then_inc(p_hi, 1)
            tiles_of_unit(4)(0)

            def norm(w, c_g, c_b):
                act.wait_ge(ln_mm, w + 1)
                act.activation(mean[:], bank[6][:, 0:S], ACT.Copy, scale=1.0 / D).then_inc(ln_mean, 1)
                for c in range(4):
                    act.wait_ge(ln_cen, 4 * w + c + 1)
                    if c >= 2:
                        act.wait_ge(ln_sqmm, 4 * w + c - 1)
                    act.activation(sq[:, c % 2], res[:, 4 * c:4 * c + 4], ACT.Square).then_inc(ln_sq, 1)
                act.wait_ge(ln_sqmm, 4 * w + 4)
                act.activation(rstd, bank[7][:, 0:S], ACT.Sqrt, scale=1.0 / D,
                               bias=par[:, C_EPS:C_EPS + 1]).then_inc(ln_std, 1)
                for t in range(DT):
                    act.wait_ge(ln_n, 4 * w + t // 4 + 1)
                    act.activation(res[:, t], res[:, t], ACT.Identity, scale=par[:, c_g + t:c_g + t + 1],
                                   bias=par[:, c_b + t:c_b + t + 1]).then_inc(ln_aff, 1)

            repeat(act, DT // 2, two_tiles(), *STD)
            norm(0, C_LN1G, C_LN1B)

            G = Count()

            def pg_tanh(i, b):
                act.wait_ge(pg_sum, G.value + 1)
                act.activation(tmp[:, b], tmp[:, b], ACT.Tanh, scale=0.5).then_inc(pg_th, 1)
                G.add()

            repeat(act, DT // 2, two_tiles(after=pg_tanh), *STD, (G, 2))

            J = Count()

            def silu_tanh(i, b):
                if b == 1:
                    act.wait_ge(cv_done, J.value + 1)
                    act.activation(th[:], cv[:, 0], ACT.Tanh, scale=0.5).then_inc(th_done, 1)
                    J.add()

            repeat(act, FT, two_tiles(after=silu_tanh), *STD, (J, 1))

            def down(final):
                def body(i):
                    n_s = 2 * U_DOWN_TILE
                    for s in range(n_s):
                        if not (final and s + AHEAD >= n_s):
                            split_hi_down(s)
                        U.add()
                        if s % U_DOWN_TILE == U_DOWN_TILE - 1:
                            read_half(s // U_DOWN_TILE)
                return body

            def split_hi_down(s):
                n = DOWN_LAST if (s + AHEAD) % U_DOWN_TILE == U_DOWN_TILE - 1 else BLK
                v, turn = (s + AHEAD) % RING, (s + AHEAD) // RING
                act.wait_ge(loaded[v], (U.value - s) * (16 // RING) + 16 * (turn + 1))
                act.wait_ge(mm_done, U.value + 1)
                act.activation(w_hi[:, v, 0:n * P], raw[:, v, 0:n * P], ACT.Copy).then_inc(hi_done, 1)

            repeat(act, DT // 2 - 1, down(False), (U, 2 * U_DOWN_TILE), (T, 2))
            down(True)(0)
            norm(1, C_LN2G, C_LN2B)

        @block.vector
        def _(dve):
            U, T, H, V = Count(), Count(), Count(), Count()
            dve.sem_inc(bank_free, 2)
            dve.sem_inc(idx_used, 2)
            dve.sem_inc(rot_done, 2)
            dve.sem_inc(o_out, 2)
            dve.sem_inc(row_added, 1)

            def step(ins):
                ins.then_inc(dve_step, 1)
                V.add()

            def steps_done():
                dve.wait_ge(dve_step, V.value)

            def sub(o, a, b):
                return dve.tensor_tensor(o, a, b, ALU.subtract)

            def stt(o, a, s, b, op0, op1):
                return dve.scalar_tensor_tensor(out=o, in0=a, scalar=s, in1=b, op0=op0, op1=op1)

            def f32(ap):
                return ap.bitcast(F32)

            def split_lo(s, n=UNIT):
                v = (s + AHEAD) % RING
                dve.wait_ge(hi_done, U.value + (AHEAD + 1))
                sub(w_lo[:, v, 0:n], raw[:, v, 0:n], f32(w_hi[:, v, 0:n])).then_inc(lo_done, 1)

            def add_half(b, o, scale=1.0):
                dve.wait_ge(half_done, H.value + 1)
                stt(o, bank[b][:, S:2 * S], scale, half[:, b % 2], ALU.mult, ALU.add).then_inc(bank_free, 1)
                H.add()
                T.add()

            def tile_done():
                dve.wait_ge(bank_free, T.value + 2)

            def two_tiles(take, before=None):
                def body(i):
                    for s in range(4):
                        split_lo(s)
                        U.add()
                        if s % 2:
                            take(i, s // 2)
                return body

            STD = ((U, 4), (T, 2), (H, 2))

            step(dve.memset(score[:], 0.0))
            for c in range(4):
                dve.wait_ge(x_hi, c + 1)
                t = slice(4 * c, 4 * c + 4)
                sub(x_hl[:, t, S:2 * S], x_raw[:, t], f32(x_hl[:, t, 0:S])).then_inc(x_lo, 1)
                if c < AHEAD:
                    dve.wait_ge(hi_done, c + 1)
                    sub(w_lo[:, c], raw[:, c], f32(w_hi[:, c])).then_inc(lo_done, 1)

            repeat(dve, N_FEAT // 2, two_tiles(lambda i, b: add_half(b, feat[:, i * 2 + b])), *STD)

            dve.wait_ge(pre_mm, 1)
            dve.wait_ge(ke_in, 16)
            for tb in range(2):
                step(dve.tensor_copy(wix[:, tb], bank[6][:, tb * P:tb * P + HEADS]))
                step(dve.tensor_copy(va[:, tb], bank[6][:, S + tb * P:S + tb * P + P]))
            step(dve.tensor_tensor(kpe[:], bank[7][:, 0:S], ke[:, K_COS:K_COS + S], ALU.mult))
            step(dve.tensor_tensor(tmp[:, 0], bank[7][:, S:2 * S], ke[:, K_SIN:K_SIN + S], ALU.mult))
            dve.wait_ge(bank_free, 2 + 4)
            step(dve.tensor_scalar(ka_s[:], feat[:, T_KA], SCALE_A, None, ALU.mult))
            steps_done()
            dve.sem_inc(pre_read, 1)
            step(dve.tensor_tensor(kpe[:], kpe[:], tmp[:, 0], ALU.add))
            steps_done()
            dve.sem_inc(pre_read, 1)

            J = Count()

            def q_and_indexer(i, b):
                add_half(b, qa[:, i * 2 + b + qa0[0]])
                if b == 0:
                    return
                for b in range(2):
                    dve.wait_ge(relu_done, 2 * J.value + 3 + b)
                    dve.wait_ge(idx_used, 2 * J.value + 2 + b)
                    for q, c0, nk in BLOCKS:
                        ins = stt(score[:, c0:c0 + nk], rel[:, b, c0:c0 + nk],
                                  wix[:, q, bass.ds(i * 2 + (qa0[0] + b), 1)],
                                  score[:, c0:c0 + nk], ALU.mult, ALU.add)
                    ins.then_inc(idx_used, 1)
                J.add()

            qa0 = [0]
            repeat(dve, 4, two_tiles(q_and_indexer), *STD, (J, 1))
            dve.wait_ge(par_in, 16)
            for n, t in enumerate((T_CQ, T_CKV)):
                dve.wait_ge(rms_std, n + 1)
                step(dve.reciprocal(c_std[:, n], c_std[:, n]))
                steps_done()
                for k in range(LT):
                    g = (C_QN, C_KVN)[n] + k
                    stt(feat[:, t + k], feat[:, t + k], par[:, g:g + 1], c_std[:, n], ALU.mult, ALU.mult
                        ).then_inc(rms_n, 1)
            for n, t in enumerate((T_CQ, T_CKV)):
                dve.wait_ge(rms_hi, n + 1)
                k = slice(LT * n, LT * n + LT)
                sub(c_hl[:, k, S:2 * S], feat[:, t:t + LT], f32(c_hl[:, k, 0:S])).then_inc(rms_lo, 1)
            qa0 = [8]
            repeat(dve, 4, two_tiles(q_and_indexer), *STD, (J, 1))

            dve.wait_ge(caus_in, 16)
            dve.wait_ge(idx_used, 2 + HEADS)
            step(dve.tensor_tensor(score[:], score[:], caus[:], ALU.add))
            steps_done()
            step(dve.tensor_copy(work[:], score[:]))

            def topk_round():
                for q, c0, nk in BLOCKS:
                    steps_done()
                    dve.memset(spare[:], 0.0)
                    step(dve.max(top8[:, q], work[:, c0:c0 + nk]))
                    steps_done()
                    dve.memset(spare[:], 0.0)
                    step(dve.match_replace(out=work[:, c0:c0 + nk], in_to_replace=top8[:, q],
                                           in_values=work[:, c0:c0 + nk], imm_value=-3e38))

            def latent_tiles(base, rounds_at):
                def body(i):
                    for s in range(4):
                        split_lo(s)
                        U.add()
                        for t in range(2):
                            add_half((2 * s + t) % 4, qk[:, i * 8 + (base + 2 * s + t)])
                        if s in rounds_at:
                            topk_round()
                return body

            repeat(dve, U_UQ // 4, latent_tiles(0, (0, 2)), (U, 4), (T, 8), (H, 8), (V, 8))
            repeat(dve, U_UK // 4, latent_tiles(24, (1,)), (U, 4), (T, 8), (H, 8), (V, 4))
            steps_done()
            gt, eq = rel[:, 0], rel[:, 1]
            for q, c0, nk in BLOCKS:
                c = slice(c0, c0 + nk)
                step(dve.tensor_scalar(gt[:, c], score[:, c], top8[:, q, 7:8], None, ALU.is_gt))
                step(dve.tensor_scalar(eq[:, c], score[:, c], top8[:, q, 7:8], None, ALU.is_equal))
            steps_done()
            for q, c0, nk in BLOCKS:
                c = slice(c0, c0 + nk)
                step(dve.tensor_reduce(cnt[:, q:q + 1], gt[:, c], AX_X, ALU.add))
                step(dve.tensor_tensor_scan(work[:, c], eq[:, c], eq[:, c], 0.0, ALU.add, ALU.max))
            steps_done()
            step(dve.tensor_scalar(cnt[:], cnt[:], -1.0, float(TOPK), ALU.mult, ALU.add))
            steps_done()
            for q, c0, nk in BLOCKS:
                c = slice(c0, c0 + nk)
                step(stt(work[:, c], work[:, c], cnt[:, q:q + 1], eq[:, c], ALU.is_le, ALU.mult))
            steps_done()
            step(dve.tensor_tensor(work[:], work[:], gt, ALU.add))
            steps_done()
            step(dve.tensor_scalar(work[:], work[:], -1.0, -NEG, ALU.add, ALU.mult))
            steps_done()
            step(dve.tensor_tensor(madd[:], work[:], caus[:], ALU.add))
            steps_done()

            R = Count()

            def values_and_rope(i):
                for s in range(4):
                    split_lo(s)
                    U.add()
                    dve.wait_ge(mm_done, U.value + 1)
                    dve.tensor_scalar(v_mla[:, :, bass.ds(i * (4 * S) + s * S, S)],
                                      bank[s % 2][:].rearrange("p (b n) -> p b n", b=2),
                                      1.0, None, ALU.mult).then_inc(bank_free, 1)
                    T.add()
                    j = i * 4 + s
                    dve.wait_ge(rot_mm, R.value + 1)
                    dve.wait_ge(rot_done, R.value + 2)
                    step(dve.tensor_tensor(tmp[:, 0], bank[4 + s % 2][:, 0:S], ke[:, K_SIN:K_SIN + S], ALU.mult))
                    step(dve.tensor_tensor(qp[:, j], qp[:, j], ke[:, K_COS:K_COS + S], ALU.mult))
                    steps_done()
                    dve.tensor_tensor(qp[:, j], qp[:, j], tmp[:, 0], ALU.add).then_inc(rot_done, 1)
                    R.add()

            repeat(dve, U_UV // 4, values_and_rope, (U, 4), (T, 4), (R, 4), (V, 8))
            dve.wait_ge(rot_done, 2 + 8)
            dve.wait_ge(bank_free, T.value + 2)
            dve.sem_inc(topk_done, 1)

            Hd = Count()
            dve.wait_ge(dist_in, 16)

            def gate_tile(b):
                dve.wait_ge(gate_th, G.value + 1)
                add_half(b, tmp[:, b])
                G.add()

            G = Count()

            def heads(i):
                for par_ in range(2):
                    h = Hd.value
                    split_lo(0)
                    U.add()
                    step(stt(bias[:], dist[:], par[:, bass.ds(i * 2 + (C_SLOPE + par_), 1)], madd[:],
                             ALU.mult, ALU.add))
                    steps_done()
                    dve.wait_ge(sc_a, h + 1)
                    step(dve.tensor_tensor(prob[:, 0], bank[2][:, 0:SC], bias[:], ALU.add))
                    dve.wait_ge(sc_b, h + 2)
                    step(dve.tensor_tensor(prob[:, 1], bank[3][:, 0:SC], caus[:], ALU.add))
                    steps_done()
                    for m in range(2):
                        for q, c0, nk in BLOCKS:
                            c = 2 * m + q
                            step(dve.tensor_reduce(mx[:, c:c + 1], prob[:, m, c0:c0 + nk], AX_X, ALU.max))
                    steps_done()
                    dve.tensor_scalar(nmx[:], mx[:], -1.0, None, ALU.mult).then_inc(nmx_ready, 1)
                    split_lo(1)
                    U.add()
                    dve.wait_ge(exp_done, 4 * h + 4)
                    step(dve.reciprocal(rsm[:], sm[:]))
                    steps_done()
                    for m in range(2):
                        for q, c0, nk in BLOCKS:
                            c = 2 * m + q
                            dve.tensor_scalar(prob[:, m, c0:c0 + nk], prob[:, m, c0:c0 + nk],
                                              rsm[:, c:c + 1], None, ALU.mult).then_inc(prob_ready, 1)
                    gate_tile(0)
                    split_lo(2)
                    U.add()
                    dve.wait_ge(tr_mm, h + 1)
                    dve.wait_ge(pv_mm, h + 1)
                    dve.tensor_copy(prob_t[:, 1], bank[5][:, 0:SC]).then_inc(pt_b, 1)
                    split_lo(3)
                    U.add()
                    dve.wait_ge(pv_mm, h + 2)
                    step(dve.tensor_scalar(qa[:, i * 2 + par_], bank[6 + par_][:, 0:S], 1.0, None, ALU.mult))
                    steps_done()
                    dve.tensor_scalar(qn[:, i * 2 + par_], bank[6 + par_][:, S:2 * S], 1.0, None, ALU.mult
                                      ).then_inc(o_out, 1)
                    gate_tile(1)
                    Hd.add()

            repeat(dve, HEADS // 2, heads, (U, 8), (T, 4), (H, 4), (Hd, 2), (G, 4), (V, 18))

            n = 0
            dve.wait_ge(o_out, HEADS + 2)
            for src, dst in ((qa, oa_hl), (qn, ob_hl)):
                for c in range(4):
                    n += 1
                    dve.wait_ge(o_hi, n)
                    t = slice(4 * c, 4 * c + 4)
                    sub(dst[:, t, S:2 * S], src[:, t], f32(dst[:, t, 0:S])).then_inc(o_lo, 1)
            dve.wait_ge(gate_th, 2 + 2 * DT)

            def split_tile(hl, j, v, done):
                step(dve.tensor_scalar(hl[:, j, 0:S], v, 1.0, None, ALU.mult))
                steps_done()
                sub(hl[:, j, S:2 * S], v, f32(hl[:, j, 0:S])).then_inc(done, 1)

            def gated(i, b):
                add_half(b, tmp[:, b], 0.5)
                tile_done()
                step(stt(tmp[:, b], gate[:, i * 2 + b], 1.0, tmp[:, b], ALU.add, ALU.mult))
                if b:
                    steps_done()
                    step(dve.tensor_tensor(merged, tmp[:, 0], tmp[:, 1], ALU.add))
                    steps_done()
                    split_tile(m_hl, i, merged, m_lo)

            repeat(dve, DT, two_tiles(gated), *STD, (V, 4))

            dve.wait_ge(p_hi, 1)
            sub(p_hl[:, :, S:2 * S], p_raw[:], f32(p_hl[:, :, 0:S])).then_inc(p_lo, 1)
            for s in range(4):
                split_lo(s)
                U.add()
                for t in range(4):
                    add_half(t, ple[:, 4 * s + t])
            dve.wait_ge(m_lo, DT)

            A = Count()

            def add_row(i, b):
                steps_done()
                dve.wait_ge(row_added, A.value + 1)
                dve.tensor_tensor(rowsum[:], rowsum[:], res[:, i * 2 + b], ALU.add).then_inc(row_added, 1)
                A.add()

            def norm(w):
                dve.wait_ge(ln_mean, w + 1)
                for c in range(4):
                    t = slice(4 * c, 4 * c + 4)
                    m = mean[:].rearrange("p (o s) -> p o s", o=1).to_broadcast([P, 4, S])
                    sub(res[:, t], res[:, t], m).then_inc(ln_cen, 1)
                dve.wait_ge(ln_std, w + 1)
                step(dve.reciprocal(rstd, rstd))
                steps_done()
                for c in range(4):
                    t = slice(4 * c, 4 * c + 4)
                    r = rstd.rearrange("p (o s) -> p o s", o=1).to_broadcast([P, 4, S])
                    dve.tensor_tensor(res[:, t], res[:, t], r, ALU.mult).then_inc(ln_n, 1)

            step(dve.memset(rowsum[:], 0.0))
            steps_done()
            dve.wait_ge(res_in, 16)

            def residual(i, b):
                add_half(b, tmp[:, b])
                tile_done()
                step(stt(res[:, i * 2 + b], res[:, i * 2 + b], ALPHA, tmp[:, b], ALU.mult, ALU.add))
                add_row(i, b)

            repeat(dve, DT // 2, two_tiles(residual), *STD, (A, 2), (V, 2))
            norm(0)
            for c in range(4):
                t = slice(4 * c, 4 * c + 4)
                dve.wait_ge(ln_aff, 4 * c + 4)
                step(dve.tensor_copy(x1_hl[:, t, 0:S], res[:, t]))
                steps_done()
                sub(x1_hl[:, t, S:2 * S], res[:, t], f32(x1_hl[:, t, 0:S])).then_inc(x1_lo, 1)

            G = Count()

            def embed(i, b):
                add_half(b, tmp[:, b])
                tile_done()
                t = i * 2 + b
                dve.tensor_scalar(tmp[:, b], tmp[:, b], par[:, bass.ds(i * 2 + (C_BPG + b), 1)], None, ALU.add
                                  ).then_inc(pg_sum, 1)
                G.add()
                dve.wait_ge(pg_th, G.value)
                step(dve.tensor_scalar(tmp[:, b], tmp[:, b], 0.5, 0.5, ALU.mult, ALU.add))
                steps_done()
                step(dve.tensor_tensor(tmp[:, b], tmp[:, b], ple[:, t], ALU.mult))
                steps_done()
                step(stt(res[:, t], res[:, t], ALPHA, tmp[:, b], ALU.mult, ALU.add))

            repeat(dve, DT // 2, two_tiles(embed), *STD, (G, 2), (V, 6))
            steps_done()

            J = Count()
            step(dve.memset(u[:, :, 0:2], 0.0))
            steps_done()

            def conv(i, b):
                w = [par[:, bass.ds(i * 8 + (C_CONV + 4 * b + k), 1)] for k in range(4)]
                add_half(b, u[:, b, 2:S + 2])
                tile_done()
                step(dve.tensor_scalar(cv[:, b], u[:, b, 2:S + 2], w[2], w[3], ALU.mult, ALU.add))
                steps_done()
                step(stt(cv[:, b], u[:, b, 1:S + 1], w[1], cv[:, b], ALU.mult, ALU.add))
                steps_done()
                if b == 0:
                    step(stt(cv[:, b], u[:, b, 0:S], w[0], cv[:, b], ALU.mult, ALU.add))
                    steps_done()
                    dve.sem_inc(cv_done, 1)
                else:
                    step(stt(cv[:, b], u[:, b, 0:S], w[0], cv[:, b], ALU.mult, ALU.add))
                    dve.wait_ge(th_done, J.value + 1)
                    step(stt(av[:], th[:], 1.0, cv[:, 0], ALU.add, ALU.mult))
                    steps_done()
                    step(stt(av[:], av[:], 0.5, cv[:, 1], ALU.mult, ALU.mult))
                    steps_done()
                    split_tile(act_hl, i, av[:], act_lo)
                    J.add()

            repeat(dve, FT, two_tiles(conv), *STD, (J, 1), (V, 9))

            step(dve.memset(rowsum[:], 0.0))

            def down(final):
                def body(i):
                    n_s = 2 * U_DOWN_TILE
                    for s in range(n_s):
                        if not (final and s + AHEAD >= n_s):
                            last = (s + AHEAD) % U_DOWN_TILE == U_DOWN_TILE - 1
                            split_lo(s, (DOWN_LAST if last else BLK) * P)
                        U.add()
                        if s % U_DOWN_TILE == U_DOWN_TILE - 1:
                            b = s // U_DOWN_TILE
                            t = i * 2 + b
                            add_half(b, tmp[:, b])
                            tile_done()
                            step(dve.tensor_tensor(res[:, t], res[:, t], tmp[:, b], ALU.add))
                            add_row(i, b)
                return body

            repeat(dve, DT // 2 - 1, down(False), (U, 2 * U_DOWN_TILE), (T, 2), (H, 2), (A, 2), (V, 2))
            down(True)(DT // 2 - 1)
            norm(1)

        @block.gpsimd
        def _(pool):
            pool.wait_ge(bank_free, 2 + 12)
            with pool.Fori(0, HEADS // 2) as j:
                pool.wait_ge(idx_mm, j + 1)
                pool.tensor_copy(qi_st[:], feat[:, j + T_QIDX]).then_inc(qi_staged, 1)
            pool.wait_ge(topk_done, 1)
            with pool.Fori(0, HEADS // 2) as i:
                for par_ in range(2):
                    pool.wait_ge(sc_b, i * 2 + (par_ + 1))
                    if par_ == 0:
                        pool.tensor_copy(qp_st[:], qp[:, i])
                    pool.tensor_copy(qa_st[:], qa[:, i * 2 + par_])
                    pool.tensor_copy(qn_st[:], qn[:, i * 2 + par_]).then_inc(q_staged, 1)
                    pool.wait_ge(pv_mm, i * 2 + (par_ + 1))
                    pool.tensor_copy(v_st[:], v_mla[:, :, bass.ds(i * (2 * HD) + par_ * HD, HD)]
                                     ).then_inc(v_staged, 1)



def feature_tiles(w_in):
    at = np.cumsum([0, HEADS * HD, HD, HD, HEADS * ROPE, ROPE, HEADS, LORA, LORA, ROPE, 2 * D])
    q_a, k_a, v_a, q_idx, k_idx, w_idx, c_q, c_kv, k_pe, gates = (
        w_in[:, a:b] for a, b in zip(at[:-1], at[1:]))
    pad = np.zeros((D, ROPE - HEADS), w_in.dtype)
    first = np.concatenate([k_idx, k_pe, w_idx, pad, k_idx, k_a, v_a, q_idx, c_q, c_kv], axis=1)
    return first, q_a, gates


def units_two_per_tile(w):
    n = w.shape[1] // P
    return w.reshape(2, BLK, P, n, P).transpose(3, 0, 2, 1, 4).reshape(2 * n, P, UNIT)


def units_of_tiles(w, per):
    k, n = w.shape[0] // P, w.shape[1] // P
    return w.reshape(k, P, n // per, per, P).transpose(2, 1, 3, 0, 4).reshape(n // per, P, UNIT)


def in_pairs(a, b):
    k = a.shape[0]
    return np.stack([a.reshape(k, -1, P), b.reshape(k, -1, P)], axis=2).reshape(k, -1)


def by_tile(v):
    return v.reshape(-1, P).T


def feature_major(a):
    return np.ascontiguousarray(a.T.reshape(-1, P, S).transpose(1, 0, 2))


def constants():
    t = np.arange(S)
    diff = t[:, None] - t[None, :]
    sc = np.concatenate([diff[0:P, 0:P], diff[P:S, 0:S]], axis=1)
    masks = np.stack([np.where(sc >= 0, 0.0, NEG), sc]).astype(np.float32)
    inv = np.float32(10000.0) ** (-np.arange(0, ROPE, 2, dtype=np.float32) / np.float32(ROPE))
    ang = inv[:, None] * t.astype(np.float32)[None, :]
    cos, sin = (np.tile(f(ang).astype(np.float32), (4, 1)) for f in (np.cos, np.sin))
    rot = np.zeros((P, P), np.float32)
    for i in range(P):
        j, r = divmod(i, ROPE)
        if r < ROPE // 2:
            rot[j * ROPE + r + ROPE // 2, i] = -1.0
        else:
            rot[j * ROPE + r - ROPE // 2, i] = 1.0
    dup = np.zeros((P, P), np.float32)
    dup_rot = np.zeros((P, P), np.float32)
    for i in range(P):
        dup[ROPE + i % ROPE, i] = 1.0
        dup_rot[ROPE:, i] = rot[i // ROPE * ROPE:i // ROPE * ROPE + ROPE, i]
    stay = np.concatenate([np.eye(P, dtype=np.float32), np.ones((P, P), np.float32)], axis=1)
    early = np.concatenate([cos, sin, rot, dup, dup_rot], axis=1)
    return masks, stay, early


def kernel(**inputs):
    import concourse.bacc as bacc
    from concourse.bass_utils import run_bass_kernel_spmd

    a = {k: np.asarray(v) for k, v in inputs.items()}
    w = {k: v[0] for k, v in a.items() if k != "x"}
    first, q_a, gates = feature_tiles(w["w_in"])
    w_uq = w["w_uq"]
    w_uq = np.concatenate([w_uq[:, :, HD:].reshape(LORA, -1), w_uq[:, :, :HD].reshape(LORA, -1)], axis=1)
    w_uv = w["w_uv"].reshape(LT, P, U_UV, S).transpose(2, 1, 0, 3).reshape(U_UV, P, UNIT)
    down = np.zeros((DT, P, U_DOWN_TILE * BLK, P), w["w_down"].dtype)
    down[:, :, 0:FT] = w["w_down"].reshape(FT, P, DT, P).transpose(2, 1, 0, 3)
    down = down.reshape(DT, P, U_DOWN_TILE, UNIT).transpose(0, 2, 1, 3).reshape(-1, P, UNIT)
    stream = np.concatenate([
        units_two_per_tile(first), units_two_per_tile(q_a),
        units_of_tiles(w_uq, 2), units_of_tiles(w["w_uk"].reshape(LORA, -1), 2), w_uv,
        units_two_per_tile(in_pairs(gates[:, :D], gates[:, D:])),
        units_two_per_tile(in_pairs(w["w_branch_a"], w["w_branch_b"])),
        units_of_tiles(w["w_pe"], 4), units_two_per_tile(w["w_o"]), units_two_per_tile(w["w_pg"]),
        units_two_per_tile(in_pairs(w["w_up"][:, :FF], w["w_up"][:, FF:])), down])
    assert stream.shape[0] == U_ALL

    conv = np.concatenate([w["conv_w"], w["conv_b"][None]])
    conv = conv.reshape(4, 2, FT, P).transpose(3, 2, 1, 0).reshape(P, -1)
    slopes = np.tile(-np.exp2(-8.0 * np.arange(1, HEADS + 1) / HEADS).astype(np.float32), (P, 1))
    eps = np.tile(np.array([LN_EPS, RMS_EPS, RMS_EPS / SCALE_B ** 2], np.float32), (P, 1))
    params = np.concatenate([conv, slopes] + [by_tile(w[n]) for n in (
        "ln1_g", "ln1_b", "ln2_g", "ln2_b", "b_pg", "q_a_norm", "kv_a_norm")] + [eps], axis=1)
    masks, stay, early = constants()
    arrays = {
        "stream": stream, "x_t": feature_major(a["x"][0]), "p_t": feature_major(w["p"][0]),
        "params": params, "consts_stay": stay, "consts_early": early, "masks": masks,
    }
    arrays = {k: np.ascontiguousarray(v) for k, v in arrays.items()}

    nc = bacc.Bacc("TRN2", target_bir_lowering=False, num_devices=1, dynamic_dma_scratch_size=1024)
    args = [nc.dram_tensor(k, v.shape, F32, kind="ExternalInput").ap() for k, v in arrays.items()]
    args.append(nc.dram_tensor("out", (P, DT, S), F32, kind="ExternalOutput").ap())
    hybrid_block(nc, *args)
    r = run_bass_kernel_spmd(nc, [arrays], core_ids=[0])
    y = np.asarray(r.results[0]["out"])
    return y.transpose(2, 1, 0).reshape(1, S, D)
```

```python
from contextlib import ExitStack

import numpy as np

import concourse.bass as bass
from concourse import mybir

F32 = mybir.dt.float32
F32R = mybir.dt.float32r
ALU = mybir.AluOpType
ACT = mybir.ActivationFunctionType
AX_X = mybir.AxisListType.X

P = 128
S = 256
D = 2048
HEADS = 16
HD = 128
ROPE = 64
LORA = 512
TOPK = 64
FF = 5632
PLE = 256
ALPHA = 2.0 ** 0.25
LN_EPS = 1e-5
RMS_EPS = 1e-6
NEG = -1e30
SCALE_A = HD ** -0.5
SCALE_B = (HD + ROPE) ** -0.5

RING = 4
AHEAD = 3
BLK = 8
UNIT = BLK * P
DT = D // P
FT = FF // P
LT = LORA // P
N_FEAT = 20
T_KIDX, T_WIDX, T_KA, T_VA, T_QIDX, T_CQ, T_CKV = 0, 1, 2, 3, 4, 12, 16
SC = P + S
BLOCKS = ((0, 0, P), (1, P, S))

U_FEAT, U_QA, U_UQ, U_UK, U_UV = 2 * N_FEAT, 2 * DT, 12, 8, 8
U_GATE, U_BRANCH, U_PLE, U_O, U_PG, U_UP = 4 * DT, 4 * DT, 4, 2 * DT, 2 * DT, 4 * FT
U_DOWN_TILE = -(-FT // BLK)
DOWN_LAST = FT - (U_DOWN_TILE - 1) * BLK
U_BEFORE_DOWN = U_FEAT + U_QA + U_UQ + U_UK + U_UV + U_GATE + U_BRANCH + U_PLE + U_O + U_PG + U_UP
U_ALL = U_BEFORE_DOWN + U_DOWN_TILE * DT

C_CONV = 0
C_SLOPE = C_CONV + 8 * FT
C_LN1G = C_SLOPE + HEADS
C_LN1B = C_LN1G + DT
C_LN2G = C_LN1B + DT
C_LN2B = C_LN2G + DT
C_BPG = C_LN2B + DT
C_QN = C_BPG + DT
C_KVN = C_QN + LT
C_EPS = C_KVN + LT
N_PAR = C_EPS + 3

K_IDENT, K_ONES = 0, P
K_STAY = 2 * P
K_COS, K_SIN, K_ROT, K_DUP, K_DUPROT = 0, S, 2 * S, 2 * S + P, 2 * S + 2 * P
K_EARLY = 2 * S + 3 * P


LN_DVE, LN_POOL = (0, 1), (2, 3)


class Count:

    def __init__(self, start=0):
        self.base, self.k = start, 0

    @property
    def value(self):
        return self.base + self.k

    def add(self, n=1):
        self.k += n


def repeat(eng, times, body, *counts):
    starts = [c.value for c, _ in counts]
    with eng.Fori(0, times) as i:
        for (c, n), s in zip(counts, starts):
            c.base, c.k = i * n + s, 0
        body(i)
        assert all(c.k == n for c, n in counts), [(c.k, n) for c, n in counts]
    for (c, n), s in zip(counts, starts):
        c.base, c.k = s + times * n, 0


def hybrid_block(nc, stream, x_t, p_t, params, consts_stay, consts_early, masks, out):
    with ExitStack() as ctx:
        def sb(name, shape, dt=F32):
            return ctx.enter_context(nc.sbuf_tensor(name, shape, dt))

        def overlay(*items):
            with ExitStack() as phase:
                return [phase.enter_context(nc.sbuf_tensor(n, s, d)) for n, s, d in items]

        def gap(name, kib):
            return (name, [P, kib * 256], F32)

        raw = sb("raw", [P, RING, UNIT])
        w_hi = sb("w_hi", [P, RING, UNIT], F32R)
        w_lo = sb("w_lo", [P, RING, UNIT], F32R)
        par = sb("par", [P, N_PAR])
        kc = sb("kc", [P, K_STAY])
        half = sb("half", [P, 2, S])
        tmp = sb("tmp", [P, 2, S])
        ident = kc[:, K_IDENT:K_IDENT + P]
        ones = kc[:, K_ONES:K_ONES + P]

        madd, dist, caus, ke, score, work, rel, qi_st, top8, cnt, spare = overlay(
            ("madd", [P, SC], F32), ("dist", [P, SC], F32), ("caus", [P, SC], F32),
            ("ke", [P, K_EARLY], F32), ("score", [P, SC], F32), ("work", [P, SC], F32),
            ("rel", [P, 2, SC], F32), ("qi_st", [P, S], F32), ("top8", [P, 2, 8], F32),
            ("cnt", [P, 2], F32), ("spare", [P, 1], F32))
        _, bias, prob, prob_t, qa_st, qn_st, qp_st, v_st, nmx, sm, rsm = overlay(
            ("masks_", [P, 3 * SC], F32), ("bias", [P, SC], F32), ("prob", [P, 2, SC], F32),
            ("prob_t", [P, 2, SC], F32), ("qa_st", [P, S], F32), ("qn_st", [P, S], F32),
            ("qp_st", [P, S], F32), ("v_st", [P, 2, HD], F32), ("nmx", [P, 2, 2], F32), ("sm", [P, 4], F32), ("rsm", [P, 4], F32))
        p_raw, p_hl, merged, sq, rows, mean, var, rstd = overlay(
            ("p_raw", [P, 2, S], F32), ("p_hl", [P, 2, 2 * S], F32R), ("merged", [P, S], F32),
            ("sq", [P, 2, S], F32), ("rows", [P, 2, S], F32), ("mean", [P, S], F32),
            ("var", [P, S], F32), ("rstd", [P, S], F32))
        sb("scratch", [P, 16 * 256 + 128])

        x_hl, qa, qk, v_mla, ka_s, kpe, va, wix, _, feat, c_hl = overlay(
            ("x_hl", [P, DT, 2 * S], F32R), ("qa", [P, DT, S], F32),
            ("qk", [P, 40, S], F32), ("v_mla", [P, 2, D], F32),
            ("ka_s", [P, S], F32), ("kpe", [P, S], F32), ("va", [P, 2, HD], F32),
            ("wix", [P, 2, HEADS], F32), gap("g1", 2),
            ("feat", [P, N_FEAT, S], F32), ("c_hl", [P, 2 * LT, 2 * S], F32R))
        qp, qn, kn = (qk[:, a:b] for a, b in ((0, 8), (8, 24), (24, 40)))
        _, x_raw = overlay(gap("g2", 88), ("x_raw", [P, DT, S], F32))
        _, c_sq, c_std = overlay(gap("g2b", 88), ("c_sq", [P, 2, LT, S], F32), ("c_std", [P, 2, S], F32))
        oa_hl, m_hl, _, ob_hl, _, gate = overlay(
            ("oa_hl", [P, DT, 2 * S], F32R), ("m_hl", [P, DT, 2 * S], F32R), gap("g3", 8),
            ("ob_hl", [P, DT, 2 * S], F32R), gap("g4", 5), ("gate", [P, 2 * DT, S], F32))
        res, _, ple = overlay(("res", [P, DT, S], F32), gap("g5", 95), ("ple", [P, DT, S], F32))
        _, x1_hl = overlay(gap("g6", 16), ("x1_hl", [P, DT, 2 * S], F32R))
        _, act_hl, u, cv, th, sig, av = overlay(
            gap("g7", 48), ("act_hl", [P, FT, 2 * S], F32R), ("u", [P, 2, S + 2], F32),
            ("cv", [P, 2, S], F32), ("th", [P, S], F32), ("sig", [P, S], F32), ("av", [P, S], F32))

        bank = [ctx.enter_context(nc.psum_tensor(f"bank{i}", [P, 2 * S], F32)) for i in range(8)]

        def sem(name):
            return ctx.enter_context(nc.semaphore(name))

        loaded = [sem(f"loaded{s}") for s in range(RING)]
        hi_done = sem("hi_done")
        lo_done = sem("lo_done")
        mm_done = sem("mm_done")
        half_done = sem("half_done")
        bank_free = sem("bank_free")
        par_in, kc_in, ke_in, caus_in, dist_in, p_in, res_in = (sem(n) for n in (
            "par_in", "kc_in", "ke_in", "caus_in", "dist_in", "p_in", "res_in"))
        x_in = [sem(f"x_in{c}") for c in range(4)]
        x_hi, x_lo = sem("x_hi"), sem("x_lo")
        pre_mm, pre_read = sem("pre_mm"), sem("pre_read")
        qi_staged, idx_mm, relu_done, idx_used = (sem(n) for n in (
            "qi_staged", "idx_mm", "relu_done", "idx_used"))
        rms_sq, rms_mm, rms_std, rms_n, rms_hi, rms_lo = (sem(n) for n in (
            "rms_sq", "rms_mm", "rms_std", "rms_n", "rms_hi", "rms_lo"))
        rot_mm, rot_read, rot_mul, rot_done = (sem(n) for n in (
            "rot_mm", "rot_read", "rot_mul", "rot_done"))
        q_staged, v_staged, sc_a, sc_b, nmx_ready, exp_done, prob_ready = (sem(n) for n in (
            "q_staged", "v_staged", "sc_a", "sc_b", "nmx_ready", "exp_done", "prob_ready"))
        tr_mm, pt_a, pt_b, pv_mm, o_out, gate_th = (sem(n) for n in (
            "tr_mm", "pt_a", "pt_b", "pv_mm", "o_out", "gate_th"))
        o_hi, o_lo, m_lo, p_hi, p_lo = (sem(n) for n in ("o_hi", "o_lo", "m_lo", "p_hi", "p_lo"))
        row_added = [sem("row_added"), sem("square_added")]
        res_tile, sq_done, ln_mm, ln_mean, ln_var, ln_std, ln_rstd, ln_pool, ln_aff, x1_hi, x1_lo = (
            sem(n) for n in ("res_tile", "sq_done", "ln_mm", "ln_mean", "ln_var", "ln_std", "ln_rstd",
                             "ln_pool", "ln_aff", "x1_hi", "x1_lo"))
        pg_sum, pg_th, cv_done, cv_free, th_done, sig_done, act_lo = (sem(n) for n in (
            "pg_sum", "pg_th", "cv_done", "cv_free", "th_done", "sig_done", "act_lo"))
        pool_step = sem("pool_step")
        dve_step = sem("dve_step")
        out_done = sem("out_done")

        def chunk(c):
            return res[:, 4 * c:4 * c + 4]

        def over_tiles(v):
            return v[:].rearrange("p (o s) -> p o s", o=1).to_broadcast([P, 4, S])

        block = ctx.enter_context(nc.Block())

        @block.sync
        def _(sp):
            for c in range(4):
                sp.dma_start(x_raw[:, 4 * c:4 * c + 4], x_t[:, 4 * c:4 * c + 4]).then_inc(x_in[c], 16)
                sp.dma_start(raw[:, c], stream[c]).then_inc(loaded[c], 16)
            sp.dma_start(par[:], params).then_inc(par_in, 16)
            sp.dma_start(kc[:], consts_stay).then_inc(kc_in, 16)
            sp.dma_start(ke[:], consts_early).then_inc(ke_in, 16)
            sp.dma_start(caus[:], masks[0]).then_inc(caus_in, 16)
            sp.dma_start(dist[:], masks[1]).then_inc(dist_in, 16)

            def load_four(i):
                for s in range(RING):
                    sp.wait_ge(lo_done, i * RING + (s - RING + 1))
                    sp.dma_start(raw[:, s], stream[i * RING + s]).then_inc(loaded[s], 16)

            with sp.Fori(1, U_BEFORE_DOWN // RING) as i:
                load_four(i)

            with sp.Fori(0, DT // 2) as i:
                for s in range(2 * U_DOWN_TILE):
                    n = (DOWN_LAST if s % U_DOWN_TILE == U_DOWN_TILE - 1 else BLK) * P
                    sp.wait_ge(lo_done, i * (2 * U_DOWN_TILE) + (U_BEFORE_DOWN + s - RING + 1))
                    sp.dma_start(raw[:, s % RING, 0:n],
                                 stream[i * (2 * U_DOWN_TILE) + (U_BEFORE_DOWN + s), :, 0:n]
                                 ).then_inc(loaded[s % RING], 16)

            for c in range(4):
                sp.wait_ge(ln_aff, 4 + c + 1)
                sp.dma_start(out[:, 4 * c:4 * c + 4], res[:, 4 * c:4 * c + 4]).then_inc(out_done, 16)
            sp.wait_ge(out_done, 4 * 16)

        @block.tensor
        def _(pe):
            U, T = Count(), Count()
            pe.sem_inc(mm_done, 1)
            pe.sem_inc(idx_mm, 1)
            pe.sem_inc(sc_b, 1)
            pe.sem_inc(pv_mm, 1)

            def block_mm(s, c, b, x, first, last):
                w = slice(c * P, c * P + P)
                pe.matmul(bank[b][:], w_hi[:, s, w], x, start=first, stop=False)
                return pe.matmul(bank[b][:, S:2 * S], w_lo[:, s, w], x[:, 0:S], start=False, stop=last)

            def take_unit():
                pe.wait_ge(lo_done, U.value + 1)

            def take_bank(users=2):
                pe.wait_ge(bank_free, T.value + (3 - users))

            def unit_of_tile(s, b, x, k0, n=BLK, first=False, last=False, need=None):
                take_unit()
                if first:
                    take_bank()
                for c in range(n):
                    if need:
                        need(k0 + c)
                    ins = block_mm(s, c, b, x[:, k0 + c], first and c == 0, last and c == n - 1)
                ins.then_inc(mm_done, 1)
                U.add()
                if last:
                    T.add()

            def two_tiles(xs, before=None, needs=(None, None)):
                def body(i):
                    if before:
                        before(i)
                    for s in range(4):
                        unit_of_tile(s, s // 2, xs[s // 2], BLK * (s % 2), first=s % 2 == 0,
                                     last=s % 2 == 1, need=needs[s // 2])
                return body

            def each(sem_, n, start=0):
                def need(k):
                    if k % n == 0:
                        pe.wait_ge(sem_, start + k // n + 1)
                return need

            STD = ((U, 4), (T, 2))
            x2 = (x_hl, x_hl)

            def tiles_split(sem_, start=0):
                def need(k):
                    if k % 4 == 0:
                        pe.wait_ge(sem_, k + 4 + start)
                return need

            def tiles_of_unit(x, k0, nk, per):
                def body(i):
                    for s in range(4):
                        take_unit()
                        for t in range(per):
                            b = (s * per + t) % 4
                            take_bank(4)
                            for k in range(nk):
                                ins = block_mm(s, t * nk + k, b, x[:, k0 + k], k == 0, k == nk - 1)
                            T.add()
                        ins.then_inc(mm_done, 1)
                        U.add()
                return body

            two_tiles(x2, needs=(each(x_lo, 4), None))(0)
            repeat(pe, N_FEAT // 2 - 1, two_tiles(x2), *STD)

            pe.wait_ge(kc_in, 16)
            pe.wait_ge(ke_in, 16)
            pe.wait_ge(bank_free, 2 + 4)
            for n, t in enumerate((T_WIDX, T_VA)):
                for tb in range(2):
                    pe.transpose(bank[6][:, (2 * n + tb) * P:(2 * n + tb + 1) * P],
                                 feat[:, t, tb * P:tb * P + P], ident)
            pe.matmul(bank[7][:, 0:S], ke[:, K_DUP:K_DUP + P], feat[:, T_KIDX], start=True, stop=True)
            pe.matmul(bank[7][:, S:2 * S], ke[:, K_DUPROT:K_DUPROT + P], feat[:, T_KIDX],
                      start=True, stop=True).then_inc(pre_mm, 1)

            J = Count()

            def indexer(i):
                pe.wait_ge(qi_staged, J.value + 1)
                pe.wait_ge(relu_done, 2 * J.value + 2)
                for b in range(2):
                    h = slice(ROPE * b, ROPE * b + ROPE)
                    key = feat[h, T_KIDX if b == 0 else T_WIDX]
                    for q, c0, nk in BLOCKS:
                        ins = pe.matmul(bank[4 + b][:, c0:c0 + nk], qi_st[h, q * P:q * P + P],
                                        key[:, 0:nk], start=True, stop=True)
                ins.then_inc(idx_mm, 1)
                J.add()

            pe.wait_ge(bank_free, 2 + 12)
            repeat(pe, 4, two_tiles(x2, indexer), *STD, (J, 1))
            pe.wait_ge(pre_read, 1)
            for n in range(2):
                pe.wait_ge(rms_sq, n + 1)
                for t in range(LT):
                    ins = pe.matmul(bank[6 + n][:, 0:S], ones, c_sq[:, n, t], start=t == 0, stop=t == LT - 1)
                ins.then_inc(rms_mm, 1)
            repeat(pe, 4, two_tiles(x2, indexer), *STD, (J, 1))

            pe.wait_ge(bank_free, T.value + 2)
            pe.wait_ge(rms_lo, 1)
            repeat(pe, U_UQ // 4, tiles_of_unit(c_hl, 0, LT, 2), (U, 4), (T, 8))
            pe.wait_ge(rms_lo, 2)
            repeat(pe, U_UK // 4, tiles_of_unit(c_hl, LT, LT, 2), (U, 4), (T, 8))

            def values_and_rope(i):
                for s in range(4):
                    take_unit()
                    take_bank()
                    for tb in range(2):
                        o = bank[s % 2][:, tb * S:tb * S + S]
                        for k in range(LT):
                            c_hi = c_hl[:, LT + k, tb * P:tb * P + P]
                            c_lo = c_hl[:, LT + k, S + tb * P:S + tb * P + P]
                            w = slice(k * S, k * S + S)
                            pe.matmul(o, c_hi, w_hi[:, s, w], start=k == 0, stop=False)
                            pe.matmul(o, c_hi, w_lo[:, s, w], start=False, stop=False)
                            ins = pe.matmul(o, c_lo, w_hi[:, s, w], start=False, stop=k == LT - 1)
                    ins.then_inc(mm_done, 1)
                    U.add()
                    T.add()
                    pe.wait_ge(rot_done, J.value + 1)
                    pe.matmul(bank[4 + s % 2][:, 0:S], ke[:, K_ROT:K_ROT + P],
                              qp[:, i * 4 + s], start=True, stop=True).then_inc(rot_mm, 1)
                    J.add()

            J = Count()
            pe.wait_ge(bank_free, T.value + 2)
            repeat(pe, U_UV // 4, values_and_rope, (U, 4), (T, 4), (J, 4))

            Hd = Count()

            def heads(i):
                for par_ in range(2):
                    half_ = slice(ROPE * par_, ROPE * par_ + ROPE)
                    h = Hd.value
                    pe.wait_ge(q_staged, h + 1)
                    for q, c0, nk in BLOCKS:
                        ins = pe.matmul(bank[2][:, c0:c0 + nk], qa_st[:, q * P:q * P + P], ka_s[:, 0:nk],
                                        start=True, stop=True)
                    ins.then_inc(sc_a, 1)
                    for q, c0, nk in BLOCKS:
                        pe.matmul(bank[3][:, c0:c0 + nk], qn_st[:, q * P:q * P + P],
                                  kn[:, i * 2 + par_, 0:nk], start=True, stop=False)
                        ins = pe.matmul(bank[3][:, c0:c0 + nk], qp_st[half_, q * P:q * P + P],
                                        kpe[half_, 0:nk], start=False, stop=True)
                    ins.then_inc(sc_b, 1)
                    unit_of_tile(0, 0, x_hl, 0, first=True)
                    unit_of_tile(1, 0, x_hl, BLK, last=True)
                    unit_of_tile(2, 1, x_hl, 0, first=True)
                    pe.wait_ge(prob_ready, 4 * h + 4)
                    for m in range(2):
                        for c in range(3):
                            ins = pe.transpose(bank[4 + m][:, c * P:c * P + P], prob[:, m, c * P:c * P + P], ident)
                    ins.then_inc(tr_mm, 1)
                    unit_of_tile(3, 1, x_hl, BLK, last=True)
                    pe.wait_ge(pt_a, h + 1)
                    pe.wait_ge(pt_b, h + 1)
                    pe.wait_ge(v_staged, h + 1)
                    pe.wait_ge(o_out, h + 1)
                    for m, v in enumerate((va, v_st)):
                        pe.matmul(bank[6 + par_][:, m * S:m * S + S], v[:, 0], prob_t[:, m, 0:S],
                                  start=True, stop=False)
                        ins = pe.matmul(bank[6 + par_][:, m * S + P:m * S + S], v[:, 1], prob_t[:, m, S:SC],
                                        start=False, stop=True)
                    ins.then_inc(pv_mm, 1)
                    Hd.add()

            pe.wait_ge(pre_read, 2)
            repeat(pe, HEADS // 2, heads, (U, 8), (T, 4), (Hd, 2))

            repeat(pe, DT, two_tiles((oa_hl, ob_hl), needs=(each(o_lo, 4), each(o_lo, 4, 4))), *STD)

            pe.wait_ge(bank_free, T.value + 2)
            pe.wait_ge(p_lo, 1)
            tiles_of_unit(p_hl, 0, 2, 4)(0)

            def norm_sums(w):
                for n in range(2):
                    pe.wait_ge(row_added[n], DT * (w + 1) + 2)
                    pe.matmul(bank[6 + n][:, 0:S], ones, rows[:, n], start=True, stop=True).then_inc(ln_mm, 1)

            repeat(pe, DT // 2, two_tiles((m_hl, m_hl), needs=(tiles_split(m_lo), None)), *STD)
            norm_sums(0)

            repeat(pe, DT // 2, two_tiles((x1_hl, x1_hl), needs=(each(x1_lo, 4), None)), *STD)
            repeat(pe, FT, two_tiles((x1_hl, x1_hl)), *STD)

            def down(i):
                for s in range(2 * U_DOWN_TILE):
                    t, c = divmod(s, U_DOWN_TILE)
                    lastu = c == U_DOWN_TILE - 1
                    unit_of_tile(s % RING, t, act_hl, c * BLK, DOWN_LAST if lastu else BLK,
                                 first=c == 0, last=lastu, need=tiles_split(act_lo, 1) if t == 0 else None)

            repeat(pe, DT // 2, down, (U, 2 * U_DOWN_TILE), (T, 2))
            norm_sums(1)

        @block.scalar
        def _(act):
            U, T = Count(), Count()
            act.sem_inc(relu_done, 2)
            act.sem_inc(gate_th, 2)

            def split_hi(s, n=UNIT):
                v, turn = (s + AHEAD) % RING, (s + AHEAD) // RING
                act.wait_ge(loaded[v], (U.value - s) * (16 // RING) + 16 * (turn + 1))
                act.wait_ge(mm_done, U.value + 1)
                act.activation(w_hi[:, v, 0:n], raw[:, v, 0:n], ACT.Copy).then_inc(hi_done, 1)

            def read_half(b, scale=1.0):
                act.wait_ge(mm_done, U.value + 1)
                act.wait_ge(bank_free, T.value + 1)
                act.activation(half[:, b % 2], bank[b][:, 0:S], ACT.Copy, scale=scale).then_inc(half_done, 1)
                T.add()

            def two_tiles(scale=1.0, before=None, after=None):
                def body(i):
                    for s in range(4):
                        split_hi(s)
                        U.add()
                        if s == 1 and before:
                            before(i)
                        if s % 2:
                            read_half(s // 2, scale)
                            if after:
                                after(i, s // 2)
                return body

            def tiles_of_unit(per):
                def body(i):
                    for s in range(4):
                        split_hi(s)
                        U.add()
                        for t in range(per):
                            read_half((s * per + t) % 4)
                return body

            STD = ((U, 4), (T, 2))

            for c in range(4):
                act.wait_ge(x_in[c], 16)
                act.activation(x_hl[:, 4 * c:4 * c + 4, 0:S], x_raw[:, 4 * c:4 * c + 4], ACT.Copy
                               ).then_inc(x_hi, 1)
                if c < AHEAD:
                    act.wait_ge(loaded[c], 16)
                    act.activation(w_hi[:, c], raw[:, c], ACT.Copy).then_inc(hi_done, 1)

            repeat(act, N_FEAT // 2, two_tiles(), *STD)
            for n, t in enumerate((T_CQ, T_CKV)):
                act.wait_ge(bank_free, 2 + N_FEAT)
                act.activation(c_sq[:, n], feat[:, t:t + LT], ACT.Square).then_inc(rms_sq, 1)

            J = Count()

            def indexer(i):
                act.wait_ge(idx_mm, J.value + 2)
                for b in range(2):
                    act.wait_ge(idx_used, 2 * J.value + 1 + b)
                    act.activation(rel[:, b], bank[4 + b][:, 0:SC], ACT.Relu).then_inc(relu_done, 1)
                J.add()

            repeat(act, 4, two_tiles(before=indexer), *STD, (J, 1))
            act.wait_ge(par_in, 16)
            for n in range(2):
                act.wait_ge(rms_mm, n + 1)
                k = SCALE_B ** 2 if n == 0 else 1.0
                e = C_EPS + (2 if n == 0 else 1)
                act.activation(c_std[:, n], bank[6 + n][:, 0:S], ACT.Sqrt, scale=1.0 / (LORA * k),
                               bias=par[:, e:e + 1]).then_inc(rms_std, 1)
            for n, t in enumerate((T_CQ, T_CKV)):
                act.wait_ge(rms_n, LT * (n + 1))
                act.activation(c_hl[:, LT * n:LT * n + LT, 0:S], feat[:, t:t + LT], ACT.Copy
                               ).then_inc(rms_hi, 1)
            repeat(act, 4, two_tiles(before=indexer), *STD, (J, 1))

            repeat(act, (U_UQ + U_UK) // 4, tiles_of_unit(2), (U, 4), (T, 8))

            def values(i):
                for s in range(4):
                    split_hi(s)
                    U.add()
                    act.wait_ge(rot_mm, R.value + 1)
                    act.wait_ge(rot_done, R.value + 1)
                    act.activation(tmp[:, s % 2], bank[4 + s % 2][:, 0:S], ACT.Copy).then_inc(rot_read, 1)
                    R.add()
                    act.wait_ge(mm_done, U.value + 1)
                    act.activation(v_mla[:, :, bass.ds(i * (4 * S) + s * S, S)],
                                   bank[s % 2][:].rearrange("p (b n) -> p b n", b=2), ACT.Copy
                                   ).then_inc(bank_free, 1)
                    T.add()

            R = Count()
            act.wait_ge(bank_free, T.value + 2)
            repeat(act, U_UV // 4, values, (U, 4), (T, 4), (R, 4))

            Hd = Count()

            def heads(i):
                for par_ in range(2):
                    h = Hd.value
                    split_hi(0)
                    U.add()
                    split_hi(1)
                    U.add()
                    act.wait_ge(nmx_ready, 2 * h + 2)
                    for m in range(2):
                        for q, c0, nk in BLOCKS:
                            c = 2 * m + q
                            act.activation(prob[:, m, c0:c0 + nk], prob[:, m, c0:c0 + nk], ACT.Exp,
                                           bias=nmx[:, m, q:q + 1], accum_out=sm[:, c:c + 1]).then_inc(exp_done, 1)
                    read_half(0)
                    split_hi(2)
                    U.add()
                    act.wait_ge(bank_free, T.value + 2)
                    act.activation(gate[:, i * 4 + 2 * par_], tmp[:, 0], ACT.Tanh, scale=0.5).then_inc(gate_th, 1)
                    split_hi(3)
                    U.add()
                    act.wait_ge(tr_mm, h + 1)
                    act.wait_ge(pv_mm, h + 1)
                    act.activation(prob_t[:, 0], bank[4][:, 0:SC], ACT.Copy).then_inc(pt_a, 1)
                    read_half(1)
                    act.wait_ge(bank_free, T.value + 2)
                    act.activation(gate[:, i * 4 + 2 * par_ + 1], tmp[:, 1], ACT.Tanh, scale=0.5
                                   ).then_inc(gate_th, 1)
                    Hd.add()

            repeat(act, HEADS // 2, heads, (U, 8), (T, 4), (Hd, 2))

            act.wait_ge(mm_done, U.value + 1)
            act.wait_ge(o_out, HEADS + 2)
            for src, dst in ((qa, oa_hl), (qn, ob_hl)):
                for c in range(4):
                    act.activation(dst[:, 4 * c:4 * c + 4, 0:S], src[:, 4 * c:4 * c + 4], ACT.Copy
                                   ).then_inc(o_hi, 1)
            act.wait_ge(pv_mm, HEADS + 1)
            act.dma_start(p_raw[:], p_t).then_inc(p_in, 16)
            repeat(act, DT, two_tiles(0.5), *STD)
            act.dma_start(res[:], x_t).then_inc(res_in, 16)

            act.wait_ge(p_in, 16)
            act.activation(p_hl[:, :, 0:S], p_raw[:], ACT.Copy).then_inc(p_hi, 1)
            tiles_of_unit(4)(0)

            N = Count()

            def squares(i, b):
                act.wait_ge(res_tile, N.value + 1)
                act.wait_ge(row_added[1], N.value + 1)
                act.activation(sq[:, b], res[:, i * 2 + b], ACT.Square).then_inc(sq_done, 1)
                N.add()

            def norm(w):
                act.wait_ge(ln_mm, 2 * w + 1)
                act.activation(mean[:], bank[6][:, 0:S], ACT.Copy, scale=1.0 / D).then_inc(ln_mean, 1)
                act.wait_ge(ln_var, w + 1)
                act.activation(rstd[:], rstd[:], ACT.Sqrt, bias=par[:, C_EPS:C_EPS + 1]).then_inc(ln_std, 1)

            repeat(act, DT // 2, two_tiles(after=squares), *STD, (N, 2))
            norm(0)
            for c in range(4):
                act.wait_ge(ln_aff, c + 1)
                t = slice(4 * c, 4 * c + 4)
                act.activation(x1_hl[:, t, 0:S], res[:, t], ACT.Copy).then_inc(x1_hi, 1)

            G = Count()

            def pg_tanh(i, b):
                act.wait_ge(pg_sum, G.value + 1)
                act.activation(tmp[:, b], tmp[:, b], ACT.Tanh, scale=0.5).then_inc(pg_th, 1)
                G.add()

            repeat(act, DT // 2, two_tiles(after=pg_tanh), *STD, (G, 2))

            J = Count()

            def silu_tanh(i, b):
                if b == 1:
                    act.wait_ge(cv_done, 2 * J.value + 1)
                    act.wait_ge(cv_free, J.value + 1)
                    act.activation(th[:], cv[:, 0], ACT.Tanh, scale=0.5).then_inc(th_done, 1)
                    act.wait_ge(th_done, J.value + 1)
                    act.activation(sig[:], th[:], ACT.Copy, bias=0.5, scale=0.5).then_inc(sig_done, 1)
                    J.add()

            repeat(act, FT, two_tiles(after=silu_tanh), *STD, (J, 1))

            def down(final):
                def body(i):
                    n_s = 2 * U_DOWN_TILE
                    for s in range(n_s):
                        if not (final and s + AHEAD >= n_s):
                            split_hi_down(s)
                        U.add()
                        if s % U_DOWN_TILE == U_DOWN_TILE - 1:
                            read_half(s // U_DOWN_TILE)
                            squares(i, s // U_DOWN_TILE)
                return body

            def split_hi_down(s):
                n = DOWN_LAST if (s + AHEAD) % U_DOWN_TILE == U_DOWN_TILE - 1 else BLK
                v, turn = (s + AHEAD) % RING, (s + AHEAD) // RING
                act.wait_ge(loaded[v], (U.value - s) * (16 // RING) + 16 * (turn + 1))
                act.wait_ge(mm_done, U.value + 1)
                act.activation(w_hi[:, v, 0:n * P], raw[:, v, 0:n * P], ACT.Copy).then_inc(hi_done, 1)

            repeat(act, DT // 2 - 1, down(False), (U, 2 * U_DOWN_TILE), (T, 2), (N, 2))
            down(True)(DT // 2 - 1)
            norm(1)

        @block.vector
        def _(dve):
            U, T, H, V = Count(), Count(), Count(), Count()
            dve.sem_inc(bank_free, 2)
            dve.sem_inc(idx_used, 2)
            dve.sem_inc(rot_done, 2)
            dve.sem_inc(o_out, 2)

            def step(ins):
                ins.then_inc(dve_step, 1)
                V.add()

            def steps_done():
                dve.wait_ge(dve_step, V.value)

            def sub(o, a, b):
                return dve.tensor_tensor(o, a, b, ALU.subtract)

            def stt(o, a, s, b, op0, op1):
                return dve.scalar_tensor_tensor(out=o, in0=a, scalar=s, in1=b, op0=op0, op1=op1)

            def f32(ap):
                return ap.bitcast(F32)

            def split_lo(s, n=UNIT):
                v = (s + AHEAD) % RING
                dve.wait_ge(hi_done, U.value + (AHEAD + 1))
                sub(w_lo[:, v, 0:n], raw[:, v, 0:n], f32(w_hi[:, v, 0:n])).then_inc(lo_done, 1)

            def add_half(b, o, scale=1.0):
                dve.wait_ge(half_done, H.value + 1)
                stt(o, bank[b][:, S:2 * S], scale, half[:, b % 2], ALU.mult, ALU.add).then_inc(bank_free, 1)
                H.add()
                T.add()

            def tile_done():
                dve.wait_ge(bank_free, T.value + 2)

            def two_tiles(take, before=None):
                def body(i):
                    for s in range(4):
                        split_lo(s)
                        U.add()
                        if s % 2:
                            take(i, s // 2)
                return body

            STD = ((U, 4), (T, 2), (H, 2))

            step(dve.memset(score[:], 0.0))
            for c in range(4):
                dve.wait_ge(x_hi, c + 1)
                t = slice(4 * c, 4 * c + 4)
                sub(x_hl[:, t, S:2 * S], x_raw[:, t], f32(x_hl[:, t, 0:S])).then_inc(x_lo, 1)
                if c < AHEAD:
                    dve.wait_ge(hi_done, c + 1)
                    sub(w_lo[:, c], raw[:, c], f32(w_hi[:, c])).then_inc(lo_done, 1)

            repeat(dve, N_FEAT // 2, two_tiles(lambda i, b: add_half(b, feat[:, i * 2 + b])), *STD)

            dve.wait_ge(pre_mm, 1)
            dve.wait_ge(ke_in, 16)
            for tb in range(2):
                step(dve.tensor_copy(wix[:, tb], bank[6][:, tb * P:tb * P + HEADS]))
                step(dve.tensor_copy(va[:, tb], bank[6][:, S + tb * P:S + tb * P + P]))
            step(dve.tensor_tensor(kpe[:], bank[7][:, 0:S], ke[:, K_COS:K_COS + S], ALU.mult))
            step(dve.tensor_tensor(tmp[:, 0], bank[7][:, S:2 * S], ke[:, K_SIN:K_SIN + S], ALU.mult))
            dve.wait_ge(bank_free, 2 + 4)
            step(dve.tensor_scalar(ka_s[:], feat[:, T_KA], SCALE_A, None, ALU.mult))
            steps_done()
            dve.sem_inc(pre_read, 1)
            step(dve.tensor_tensor(kpe[:], kpe[:], tmp[:, 0], ALU.add))
            steps_done()
            dve.sem_inc(pre_read, 1)

            J = Count()

            def q_and_indexer(i, b):
                add_half(b, qa[:, i * 2 + b + qa0[0]])
                if b == 0:
                    return
                for b in range(2):
                    dve.wait_ge(relu_done, 2 * J.value + 3 + b)
                    dve.wait_ge(idx_used, 2 * J.value + 2 + b)
                    for q, c0, nk in BLOCKS:
                        ins = stt(score[:, c0:c0 + nk], rel[:, b, c0:c0 + nk],
                                  wix[:, q, bass.ds(i * 2 + (qa0[0] + b), 1)],
                                  score[:, c0:c0 + nk], ALU.mult, ALU.add)
                    ins.then_inc(idx_used, 1)
                J.add()

            qa0 = [0]
            repeat(dve, 4, two_tiles(q_and_indexer), *STD, (J, 1))
            dve.wait_ge(par_in, 16)
            for n, t in enumerate((T_CQ, T_CKV)):
                dve.wait_ge(rms_std, n + 1)
                step(dve.reciprocal(c_std[:, n], c_std[:, n]))
                steps_done()
                for k in range(LT):
                    g = (C_QN, C_KVN)[n] + k
                    stt(feat[:, t + k], feat[:, t + k], par[:, g:g + 1], c_std[:, n], ALU.mult, ALU.mult
                        ).then_inc(rms_n, 1)
            for n, t in enumerate((T_CQ, T_CKV)):
                dve.wait_ge(rms_hi, n + 1)
                k = slice(LT * n, LT * n + LT)
                sub(c_hl[:, k, S:2 * S], feat[:, t:t + LT], f32(c_hl[:, k, 0:S])).then_inc(rms_lo, 1)
            qa0 = [8]
            repeat(dve, 4, two_tiles(q_and_indexer), *STD, (J, 1))

            dve.wait_ge(caus_in, 16)
            dve.wait_ge(idx_used, 2 + HEADS)
            step(dve.tensor_tensor(score[:], score[:], caus[:], ALU.add))
            steps_done()
            step(dve.tensor_copy(work[:], score[:]))

            def topk_round():
                for q, c0, nk in BLOCKS:
                    steps_done()
                    dve.memset(spare[:], 0.0)
                    step(dve.max(top8[:, q], work[:, c0:c0 + nk]))
                    steps_done()
                    dve.memset(spare[:], 0.0)
                    step(dve.match_replace(out=work[:, c0:c0 + nk], in_to_replace=top8[:, q],
                                           in_values=work[:, c0:c0 + nk], imm_value=-3e38))

            def latent_tiles(base, rounds_at):
                def body(i):
                    for s in range(4):
                        split_lo(s)
                        U.add()
                        for t in range(2):
                            add_half((2 * s + t) % 4, qk[:, i * 8 + (base + 2 * s + t)])
                        if s in rounds_at:
                            topk_round()
                return body

            repeat(dve, U_UQ // 4, latent_tiles(0, (0, 2)), (U, 4), (T, 8), (H, 8), (V, 8))
            repeat(dve, U_UK // 4, latent_tiles(24, (1,)), (U, 4), (T, 8), (H, 8), (V, 4))
            steps_done()
            gt, eq = rel[:, 0], rel[:, 1]
            for q, c0, nk in BLOCKS:
                c = slice(c0, c0 + nk)
                step(dve.tensor_scalar(gt[:, c], score[:, c], top8[:, q, 7:8], None, ALU.is_gt))
                step(dve.tensor_scalar(eq[:, c], score[:, c], top8[:, q, 7:8], None, ALU.is_equal))
            steps_done()
            for q, c0, nk in BLOCKS:
                c = slice(c0, c0 + nk)
                step(dve.tensor_reduce(cnt[:, q:q + 1], gt[:, c], AX_X, ALU.add))
                step(dve.tensor_tensor_scan(work[:, c], eq[:, c], eq[:, c], 0.0, ALU.add, ALU.max))
            steps_done()
            step(dve.tensor_scalar(cnt[:], cnt[:], -1.0, float(TOPK), ALU.mult, ALU.add))
            steps_done()
            for q, c0, nk in BLOCKS:
                c = slice(c0, c0 + nk)
                step(stt(work[:, c], work[:, c], cnt[:, q:q + 1], eq[:, c], ALU.is_le, ALU.mult))
            steps_done()
            step(dve.tensor_tensor(work[:], work[:], gt, ALU.add))
            steps_done()
            step(dve.tensor_scalar(work[:], work[:], -1.0, -NEG, ALU.add, ALU.mult))
            steps_done()
            step(dve.tensor_tensor(madd[:], work[:], caus[:], ALU.add))
            steps_done()

            def values(i):
                for s in range(4):
                    split_lo(s)
                    U.add()
                    T.add()
                    j = i * 4 + s
                    dve.wait_ge(rot_mul, 2 * R.value + 2)
                    dve.tensor_tensor(qp[:, j], qp[:, j], tmp[:, s % 2], ALU.add).then_inc(rot_done, 1)
                    R.add()

            R = Count()
            repeat(dve, U_UV // 4, values, (U, 4), (T, 4), (R, 4))

            Hd = Count()
            dve.wait_ge(dist_in, 16)

            def gate_tile(b):
                dve.wait_ge(gate_th, G.value + 1)
                add_half(b, tmp[:, b])
                G.add()

            G = Count()

            def heads(i):
                for par_ in range(2):
                    h = Hd.value
                    split_lo(0)
                    U.add()
                    step(stt(bias[:], dist[:], par[:, bass.ds(i * 2 + (C_SLOPE + par_), 1)], madd[:],
                             ALU.mult, ALU.add))
                    steps_done()
                    dve.wait_ge(sc_a, h + 1)
                    step(dve.tensor_tensor(prob[:, 0], bank[2][:, 0:SC], bias[:], ALU.add))
                    dve.wait_ge(sc_b, h + 2)
                    step(dve.tensor_tensor(prob[:, 1], bank[3][:, 0:SC], caus[:], ALU.add))
                    steps_done()
                    for q, c0, nk in BLOCKS:
                        dve.tensor_reduce(nmx[:, :, q], prob[:, :, c0:c0 + nk], AX_X, ALU.max, negate=True
                                          ).then_inc(nmx_ready, 1)
                    split_lo(1)
                    U.add()
                    dve.wait_ge(exp_done, 4 * h + 4)
                    step(dve.reciprocal(rsm[:], sm[:]))
                    steps_done()
                    for m in range(2):
                        for q, c0, nk in BLOCKS:
                            c = 2 * m + q
                            dve.tensor_scalar(prob[:, m, c0:c0 + nk], prob[:, m, c0:c0 + nk],
                                              rsm[:, c:c + 1], None, ALU.mult).then_inc(prob_ready, 1)
                    gate_tile(0)
                    split_lo(2)
                    U.add()
                    dve.wait_ge(tr_mm, h + 1)
                    dve.wait_ge(pv_mm, h + 1)
                    dve.tensor_copy(prob_t[:, 1], bank[5][:, 0:SC]).then_inc(pt_b, 1)
                    split_lo(3)
                    U.add()
                    gate_tile(1)
                    dve.wait_ge(pv_mm, h + 2)
                    step(dve.tensor_scalar(qa[:, i * 2 + par_], bank[6 + par_][:, 0:S], 1.0, None, ALU.mult))
                    steps_done()
                    dve.tensor_scalar(qn[:, i * 2 + par_], bank[6 + par_][:, S:2 * S], 1.0, None, ALU.mult
                                      ).then_inc(o_out, 1)
                    Hd.add()

            repeat(dve, HEADS // 2, heads, (U, 8), (T, 4), (H, 4), (Hd, 2), (G, 4), (V, 10))

            n = 0
            dve.wait_ge(o_out, HEADS + 2)
            for src, dst in ((qa, oa_hl), (qn, ob_hl)):
                for c in range(4):
                    n += 1
                    dve.wait_ge(o_hi, n)
                    t = slice(4 * c, 4 * c + 4)
                    sub(dst[:, t, S:2 * S], src[:, t], f32(dst[:, t, 0:S])).then_inc(o_lo, 1)
            dve.wait_ge(gate_th, 2 + 2 * DT)

            def split_tile(hl, j, v, done):
                step(dve.tensor_scalar(hl[:, j, 0:S], v, 1.0, None, ALU.mult))
                steps_done()
                sub(hl[:, j, S:2 * S], v, f32(hl[:, j, 0:S])).then_inc(done, 1)

            def gated(i, b):
                add_half(b, tmp[:, b], 0.5)
                tile_done()
                step(stt(tmp[:, b], gate[:, i * 2 + b], 1.0, tmp[:, b], ALU.add, ALU.mult))
                if b:
                    steps_done()
                    step(dve.tensor_tensor(merged[:], tmp[:, 0], tmp[:, 1], ALU.add))
                    steps_done()
                    split_tile(m_hl, i, merged[:], m_lo)

            repeat(dve, DT, two_tiles(gated), *STD, (V, 4))

            dve.wait_ge(p_hi, 1)
            sub(p_hl[:, :, S:2 * S], p_raw[:], f32(p_hl[:, :, 0:S])).then_inc(p_lo, 1)
            for s in range(4):
                split_lo(s)
                U.add()
                for t in range(4):
                    add_half(t, ple[:, 4 * s + t])
            dve.wait_ge(m_lo, DT)

            def norm(w, c_g, c_b):
                dve.wait_ge(ln_mean, w + 1)
                step(dve.tensor_tensor(var[:], mean[:], mean[:], ALU.mult))
                steps_done()
                dve.wait_ge(ln_mm, 2 * w + 2)
                step(stt(var[:], bank[7][:, 0:S], 1.0 / D, var[:], ALU.mult, ALU.subtract))
                steps_done()
                dve.tensor_scalar(rstd[:], var[:], 0.0, None, ALU.max).then_inc(ln_var, 1)
                for c in LN_DVE:
                    step(sub(chunk(c), chunk(c), over_tiles(mean)))
                dve.wait_ge(ln_std, w + 1)
                step(dve.reciprocal(rstd[:], rstd[:]))
                steps_done()
                dve.sem_inc(ln_rstd, 1)
                for c in range(4):
                    if c in LN_DVE:
                        step(dve.tensor_tensor(chunk(c), chunk(c), over_tiles(rstd), ALU.mult))
                        steps_done()
                    else:
                        dve.wait_ge(ln_pool, 2 * w + c - 1)
                    for t in range(4 * c, 4 * c + 4):
                        step(dve.tensor_scalar(res[:, t], res[:, t], par[:, c_g + t:c_g + t + 1],
                                               par[:, c_b + t:c_b + t + 1], ALU.mult, ALU.add))
                    steps_done()
                    dve.sem_inc(ln_aff, 1)
                    if w == 0 and c:
                        x1_split(c - 1)
                if w == 0:
                    x1_split(3)

            def x1_split(c):
                dve.wait_ge(x1_hi, c + 1)
                t = slice(4 * c, 4 * c + 4)
                sub(x1_hl[:, t, S:2 * S], res[:, t], f32(x1_hl[:, t, 0:S])).then_inc(x1_lo, 1)

            dve.wait_ge(res_in, 16)

            def residual(i, b):
                add_half(b, tmp[:, b])
                tile_done()
                stt(res[:, i * 2 + b], res[:, i * 2 + b], ALPHA, tmp[:, b], ALU.mult, ALU.add).then_inc(res_tile, 1)

            repeat(dve, DT // 2, two_tiles(residual), *STD)
            norm(0, C_LN1G, C_LN1B)

            G = Count()

            def embed(i, b):
                add_half(b, tmp[:, b])
                tile_done()
                t = i * 2 + b
                dve.tensor_scalar(tmp[:, b], tmp[:, b], par[:, bass.ds(i * 2 + (C_BPG + b), 1)], None, ALU.add
                                  ).then_inc(pg_sum, 1)
                G.add()
                dve.wait_ge(pg_th, G.value)
                step(dve.tensor_scalar(tmp[:, b], tmp[:, b], 0.5, 0.5, ALU.mult, ALU.add))
                steps_done()
                step(dve.tensor_tensor(tmp[:, b], tmp[:, b], ple[:, t], ALU.mult))
                steps_done()
                step(stt(res[:, t], res[:, t], ALPHA, tmp[:, b], ALU.mult, ALU.add))

            repeat(dve, DT // 2, two_tiles(embed), *STD, (G, 2), (V, 6))
            steps_done()

            J = Count()
            step(dve.memset(u[:, :, 0:2], 0.0))
            steps_done()

            def conv(i, b):
                w = [par[:, bass.ds(i * 8 + (C_CONV + 4 * b + k), 1)] for k in range(4)]
                add_half(b, u[:, b, 2:S + 2])
                tile_done()
                dve.wait_ge(cv_free, J.value + 1)
                step(dve.tensor_scalar(cv[:, b], u[:, b, 2:S + 2], w[2], w[3], ALU.mult, ALU.add))
                steps_done()
                step(stt(cv[:, b], u[:, b, 1:S + 1], w[1], cv[:, b], ALU.mult, ALU.add))
                steps_done()
                stt(cv[:, b], u[:, b, 0:S], w[0], cv[:, b], ALU.mult, ALU.add).then_inc(cv_done, 1)
                if b == 1:
                    J.add()

            repeat(dve, FT, two_tiles(conv), *STD, (J, 1), (V, 4))


            def down(final):
                def body(i):
                    n_s = 2 * U_DOWN_TILE
                    for s in range(n_s):
                        if not (final and s + AHEAD >= n_s):
                            last = (s + AHEAD) % U_DOWN_TILE == U_DOWN_TILE - 1
                            split_lo(s, (DOWN_LAST if last else BLK) * P)
                        U.add()
                        if s % U_DOWN_TILE == U_DOWN_TILE - 1:
                            b = s // U_DOWN_TILE
                            t = i * 2 + b
                            add_half(b, tmp[:, b])
                            tile_done()
                            dve.tensor_tensor(res[:, t], res[:, t], tmp[:, b], ALU.add).then_inc(res_tile, 1)
                return body

            repeat(dve, DT // 2 - 1, down(False), (U, 2 * U_DOWN_TILE), (T, 2), (H, 2))
            down(True)(DT // 2 - 1)
            norm(1, C_LN2G, C_LN2B)

        @block.gpsimd
        def _(pool):
            pool.sem_inc(row_added[0], 2)
            pool.sem_inc(row_added[1], 2)
            pool.wait_ge(bank_free, 2 + 12)
            with pool.Fori(0, HEADS // 2) as j:
                pool.wait_ge(idx_mm, j + 1)
                pool.tensor_copy(qi_st[:], feat[:, j + T_QIDX]).then_inc(qi_staged, 1)

            V, R = Count(), Count()
            pool.wait_ge(ke_in, 16)

            def step(ins):
                ins.then_inc(pool_step, 1)
                V.add()

            def steps_done():
                pool.wait_ge(pool_step, V.value)

            def rope(i):
                for s in range(4):
                    j = i * 4 + s
                    pool.wait_ge(rot_read, R.value + 1)
                    pool.tensor_tensor(tmp[:, s % 2], tmp[:, s % 2], ke[:, K_SIN:K_SIN + S], ALU.mult
                                       ).then_inc(rot_mul, 1)
                    pool.tensor_tensor(qp[:, j], qp[:, j], ke[:, K_COS:K_COS + S], ALU.mult
                                       ).then_inc(rot_mul, 1)
                    R.add()

            repeat(pool, U_UV // 4, rope, (R, 4))
            pool.wait_ge(rot_done, 2 + 8)
            pool.wait_ge(bank_free, 2 + N_FEAT + DT + 40 + U_UV)

            with pool.Fori(0, HEADS // 2) as i:
                for par_ in range(2):
                    pool.wait_ge(sc_b, i * 2 + (par_ + 1))
                    if par_ == 0:
                        pool.tensor_copy(qp_st[:], qp[:, i])
                    pool.tensor_copy(qa_st[:], qa[:, i * 2 + par_])
                    pool.tensor_copy(qn_st[:], qn[:, i * 2 + par_]).then_inc(q_staged, 1)
                    pool.wait_ge(pv_mm, i * 2 + (par_ + 1))
                    pool.tensor_copy(v_st[:], v_mla[:, :, bass.ds(i * (2 * HD) + par_ * HD, HD)]
                                     ).then_inc(v_staged, 1)

            A = Count()

            def add_rows(i):
                for b in range(2):
                    for n, (done, new) in enumerate(((res_tile, res[:, i * 2 + b]), (sq_done, sq[:, b]))):
                        pool.wait_ge(row_added[n], A.value + 2)
                        pool.wait_ge(done, A.value + 1)
                        pool.tensor_tensor(rows[:, n], rows[:, n], new, ALU.add).then_inc(row_added[n], 1)
                    A.add()

            def clear_rows():
                step(pool.memset(rows[:], 0.0))
                steps_done()

            def norm(w):
                pool.wait_ge(ln_mean, w + 1)
                for c in LN_POOL:
                    step(pool.tensor_tensor(chunk(c), chunk(c), over_tiles(mean), ALU.subtract))
                steps_done()
                pool.wait_ge(ln_rstd, w + 1)
                for c in LN_POOL:
                    pool.tensor_tensor(chunk(c), chunk(c), over_tiles(rstd), ALU.mult).then_inc(ln_pool, 1)

            pool.wait_ge(m_lo, DT)
            clear_rows()
            repeat(pool, DT // 2, add_rows, (A, 2))
            norm(0)

            J = Count()
            pool.sem_inc(cv_free, 1)
            pool.sem_inc(act_lo, 1)

            def activate(j):
                pool.wait_ge(act_lo, J.value + 1)
                pool.wait_ge(sig_done, J.value + 1)
                step(pool.tensor_tensor(av[:], sig[:], cv[:, 0], ALU.mult))
                pool.wait_ge(cv_done, 2 * J.value + 2)
                steps_done()
                step(pool.tensor_tensor(av[:], av[:], cv[:, 1], ALU.mult))
                steps_done()
                pool.sem_inc(cv_free, 1)
                step(pool.tensor_copy(act_hl[:, j, 0:S], av[:]))
                steps_done()
                pool.tensor_tensor(act_hl[:, j, S:2 * S], av[:], act_hl[:, j, 0:S].bitcast(F32), ALU.subtract
                                   ).then_inc(act_lo, 1)
                J.add()

            repeat(pool, FT, activate, (J, 1), (V, 3))
            clear_rows()
            repeat(pool, DT // 2, add_rows, (A, 2))
            norm(1)





def feature_tiles(w_in):
    at = np.cumsum([0, HEADS * HD, HD, HD, HEADS * ROPE, ROPE, HEADS, LORA, LORA, ROPE, 2 * D])
    q_a, k_a, v_a, q_idx, k_idx, w_idx, c_q, c_kv, k_pe, gates = (
        w_in[:, a:b] for a, b in zip(at[:-1], at[1:]))
    pad = np.zeros((D, ROPE - HEADS), w_in.dtype)
    first = np.concatenate([k_idx, k_pe, w_idx, pad, k_idx, k_a, v_a, q_idx, c_q, c_kv], axis=1)
    return first, q_a, gates


def units_two_per_tile(w):
    n = w.shape[1] // P
    return w.reshape(2, BLK, P, n, P).transpose(3, 0, 2, 1, 4).reshape(2 * n, P, UNIT)


def units_of_tiles(w, per):
    k, n = w.shape[0] // P, w.shape[1] // P
    return w.reshape(k, P, n // per, per, P).transpose(2, 1, 3, 0, 4).reshape(n // per, P, UNIT)


def in_pairs(a, b):
    k = a.shape[0]
    return np.stack([a.reshape(k, -1, P), b.reshape(k, -1, P)], axis=2).reshape(k, -1)


def by_tile(v):
    return v.reshape(-1, P).T


def feature_major(a):
    return np.ascontiguousarray(a.T.reshape(-1, P, S).transpose(1, 0, 2))


def constants():
    t = np.arange(S)
    diff = t[:, None] - t[None, :]
    sc = np.concatenate([diff[0:P, 0:P], diff[P:S, 0:S]], axis=1)
    masks = np.stack([np.where(sc >= 0, 0.0, NEG), sc]).astype(np.float32)
    inv = np.float32(10000.0) ** (-np.arange(0, ROPE, 2, dtype=np.float32) / np.float32(ROPE))
    ang = inv[:, None] * t.astype(np.float32)[None, :]
    cos, sin = (np.tile(f(ang).astype(np.float32), (4, 1)) for f in (np.cos, np.sin))
    rot = np.zeros((P, P), np.float32)
    for i in range(P):
        j, r = divmod(i, ROPE)
        if r < ROPE // 2:
            rot[j * ROPE + r + ROPE // 2, i] = -1.0
        else:
            rot[j * ROPE + r - ROPE // 2, i] = 1.0
    dup = np.zeros((P, P), np.float32)
    dup_rot = np.zeros((P, P), np.float32)
    for i in range(P):
        dup[ROPE + i % ROPE, i] = 1.0
        dup_rot[ROPE:, i] = rot[i // ROPE * ROPE:i // ROPE * ROPE + ROPE, i]
    stay = np.concatenate([np.eye(P, dtype=np.float32), np.ones((P, P), np.float32)], axis=1)
    early = np.concatenate([cos, sin, rot, dup, dup_rot], axis=1)
    return masks, stay, early


def kernel(**inputs):
    import concourse.bacc as bacc
    from concourse.bass_utils import run_bass_kernel_spmd

    a = {k: np.asarray(v) for k, v in inputs.items()}
    w = {k: v[0] for k, v in a.items() if k != "x"}
    first, q_a, gates = feature_tiles(w["w_in"])
    w_uq = w["w_uq"]
    w_uq = np.concatenate([w_uq[:, :, HD:].reshape(LORA, -1), w_uq[:, :, :HD].reshape(LORA, -1)], axis=1)
    w_uv = w["w_uv"].reshape(LT, P, U_UV, S).transpose(2, 1, 0, 3).reshape(U_UV, P, UNIT)
    down = np.zeros((DT, P, U_DOWN_TILE * BLK, P), w["w_down"].dtype)
    down[:, :, 0:FT] = w["w_down"].reshape(FT, P, DT, P).transpose(2, 1, 0, 3)
    down = down.reshape(DT, P, U_DOWN_TILE, UNIT).transpose(0, 2, 1, 3).reshape(-1, P, UNIT)
    stream = np.concatenate([
        units_two_per_tile(first), units_two_per_tile(q_a),
        units_of_tiles(w_uq, 2), units_of_tiles(w["w_uk"].reshape(LORA, -1), 2), w_uv,
        units_two_per_tile(in_pairs(gates[:, :D], gates[:, D:])),
        units_two_per_tile(in_pairs(w["w_branch_a"], w["w_branch_b"])),
        units_of_tiles(w["w_pe"], 4), units_two_per_tile(w["w_o"]), units_two_per_tile(w["w_pg"]),
        units_two_per_tile(in_pairs(w["w_up"][:, :FF], w["w_up"][:, FF:])), down])
    assert stream.shape[0] == U_ALL

    conv = np.concatenate([w["conv_w"], w["conv_b"][None]])
    conv = conv.reshape(4, 2, FT, P).transpose(3, 2, 1, 0).reshape(P, -1)
    slopes = np.tile(-np.exp2(-8.0 * np.arange(1, HEADS + 1) / HEADS).astype(np.float32), (P, 1))
    eps = np.tile(np.array([LN_EPS, RMS_EPS, RMS_EPS / SCALE_B ** 2], np.float32), (P, 1))
    params = np.concatenate([conv, slopes] + [by_tile(w[n]) for n in (
        "ln1_g", "ln1_b", "ln2_g", "ln2_b", "b_pg", "q_a_norm", "kv_a_norm")] + [eps], axis=1)
    masks, stay, early = constants()
    arrays = {
        "stream": stream, "x_t": feature_major(a["x"][0]), "p_t": feature_major(w["p"][0]),
        "params": params, "consts_stay": stay, "consts_early": early, "masks": masks,
    }
    arrays = {k: np.ascontiguousarray(v) for k, v in arrays.items()}

    nc = bacc.Bacc("TRN2", target_bir_lowering=False, num_devices=1, dynamic_dma_scratch_size=1024)
    args = [nc.dram_tensor(k, v.shape, F32, kind="ExternalInput").ap() for k, v in arrays.items()]
    args.append(nc.dram_tensor("out", (P, DT, S), F32, kind="ExternalOutput").ap())
    hybrid_block(nc, *args)
    r = run_bass_kernel_spmd(nc, [arrays], core_ids=[0])
    y = np.asarray(r.results[0]["out"])
    return y.transpose(2, 1, 0).reshape(1, S, D)
```

```python
from contextlib import ExitStack

import numpy as np

import concourse.bass as bass
from concourse import mybir

F32 = mybir.dt.float32
F32R = mybir.dt.float32r
ALU = mybir.AluOpType
ACT = mybir.ActivationFunctionType
AX_X = mybir.AxisListType.X

P = 128
S = 256
D = 2048
HEADS = 16
HD = 128
ROPE = 64
LORA = 512
TOPK = 64
FF = 5632
PLE = 256
ALPHA = 2.0 ** 0.25
LN_EPS = 1e-5
RMS_EPS = 1e-6
NEG = -1e30
SCALE_A = HD ** -0.5
SCALE_B = (HD + ROPE) ** -0.5

RING = 4
TURNS = (2, 3)
AHEAD = 3
BLK = 8
UNIT = BLK * P
DT = D // P
FT = FF // P
LT = LORA // P
N_FEAT = 20
T_KIDX, T_WIDX, T_KA, T_VA, T_QIDX, T_CQ, T_CKV = 0, 1, 2, 3, 4, 12, 16
SC = P + S
BLOCKS = ((0, 0, P), (1, P, S))

U_FEAT, U_QA, U_UQ, U_UK, U_UV = 2 * N_FEAT, 2 * DT, 12, 8, 8
U_GATE, U_BRANCH, U_O, U_PLE, U_PG, U_UP = 4 * DT, 4 * DT, 2 * DT, 4, 2 * DT, 4 * FT
U_DOWN_TILE = -(-FT // BLK)
DOWN_LAST = FT - (U_DOWN_TILE - 1) * BLK
U_BEFORE_DOWN = U_FEAT + U_QA + U_UQ + U_UK + U_UV + U_GATE + U_BRANCH + U_O + U_PLE + U_PG + U_UP
U_ALL = U_BEFORE_DOWN + U_DOWN_TILE * DT

C_CONV = 0
C_SLOPE = C_CONV + 8 * FT
C_LN1G = C_SLOPE + HEADS
C_LN1B = C_LN1G + DT
C_LN2G = C_LN1B + DT
C_LN2B = C_LN2G + DT
C_BPG = C_LN2B + DT
C_QN = C_BPG + DT
C_KVN = C_QN + LT
C_EPS = C_KVN + LT
N_PAR = C_EPS + 3

K_IDENT, K_MEAN = 0, P
K_STAY = 2 * P
K_COS, K_SIN, K_ROT, K_DUP, K_DUPROT = 0, S, 2 * S, 2 * S + P, 2 * S + 2 * P
K_EARLY = 2 * S + 3 * P

FIRST_LOADS = (("x", 0), ("w", 0), ("x", 1), ("x", 2), ("w", 1), ("x", 3), ("w", 2), ("w", AHEAD))

GRAN = 2
NG = DT // GRAN
LN_DVE, LN_POOL = range(0, 4), range(4, NG)


class Count:

    def __init__(self, start=0):
        self.base, self.k = start, 0

    @property
    def value(self):
        return self.base + self.k

    def add(self, n=1):
        self.k += n


def repeat(eng, times, body, *counts):
    starts = [c.value for c, _ in counts]
    with eng.Fori(0, times) as i:
        for (c, n), s in zip(counts, starts):
            c.base, c.k = i * n + s, 0
        body(i)
        assert all(c.k == n for c, n in counts), [(c.k, n) for c, n in counts]
    for (c, n), s in zip(counts, starts):
        c.base, c.k = s + times * n, 0


def hybrid_block(nc, stream, x_t, p_t, params, consts_stay, consts_early, masks, out):
    with ExitStack() as ctx:
        def sb(name, shape, dt=F32):
            return ctx.enter_context(nc.sbuf_tensor(name, shape, dt))

        def overlay(*items):
            with ExitStack() as phase:
                return [phase.enter_context(nc.sbuf_tensor(n, s, d)) for n, s, d in items]

        def gap(name, kib):
            return (name, [P, kib * 256], F32)

        raw = sb("raw", [P, RING, UNIT])
        w_hi = sb("w_hi", [P, RING, UNIT], F32R)
        w_lo = sb("w_lo", [P, RING, UNIT], F32R)
        par = sb("par", [P, N_PAR])
        kc = sb("kc", [P, K_STAY])
        half = sb("half", [P, 2, S])
        tmp = sb("tmp", [P, 2, S])
        ident = kc[:, K_IDENT:K_IDENT + P]
        mean_of = kc[:, K_MEAN:K_MEAN + P]

        madd, dist, caus, ke, score, work, rel, qi_st, top8, cnt, spare = overlay(
            ("madd", [P, SC], F32), ("dist", [P, SC], F32), ("caus", [P, SC], F32),
            ("ke", [P, K_EARLY], F32), ("score", [P, SC], F32), ("work", [P, SC], F32),
            ("rel", [P, 2, SC], F32), ("qi_st", [P, S], F32), ("top8", [P, 2, 8], F32),
            ("cnt", [P, 2], F32), ("spare", [P, 1], F32))
        _, bias, prob, prob_t, qa_st, qn_st, qp_st, v_st, nmx, sm, rsm = overlay(
            ("masks_", [P, 3 * SC], F32), ("bias", [P, SC], F32), ("prob", [P, 2, SC], F32),
            ("prob_t", [P, 2, SC], F32), ("qa_st", [P, S], F32), ("qn_st", [P, S], F32),
            ("qp_st", [P, S], F32), ("v_st", [P, 2, HD], F32), ("nmx", [P, 2, 2], F32),
            ("sm", [P, 4], F32), ("rsm", [P, 4], F32))
        p_raw, p_hl, merged, sq, rows, eps_std, mean, var, rstd = overlay(
            ("p_raw", [P, 2, S], F32), ("p_hl", [P, 2, 2 * S], F32R), ("merged", [P, S], F32),
            ("sq", [P, 2, S], F32), ("rows", [P, 2, S], F32), ("eps_std", [P, 1], F32), ("mean", [P, S], F32),
            ("var", [P, S], F32), ("rstd", [P, S], F32))
        sb("scratch", [P, 16 * 256 + 128])

        x_hl, qa, qk, v_mla, ka_s, kpe, va, wix, _, feat, c_hl = overlay(
            ("x_hl", [P, DT, 2 * S], F32R), ("qa", [P, DT, S], F32),
            ("qk", [P, 40, S], F32), ("v_mla", [P, 2, D], F32),
            ("ka_s", [P, S], F32), ("kpe", [P, S], F32), ("va", [P, 2, HD], F32),
            ("wix", [P, 2, HEADS], F32), gap("g1", 2),
            ("feat", [P, N_FEAT, S], F32), ("c_hl", [P, 2 * LT, 2 * S], F32R))
        qp, qn, kn = (qk[:, a:b] for a, b in ((0, 8), (8, 24), (24, 40)))
        _, x_raw = overlay(gap("g2", 88), ("x_raw", [P, DT, S], F32))
        _, c_sq, c_std = overlay(gap("g2b", 88), ("c_sq", [P, 2, LT, S], F32), ("c_std", [P, 2, S], F32))
        oa_hl, m_hl, _, ob_hl, _, gate = overlay(
            ("oa_hl", [P, DT, 2 * S], F32R), ("m_hl", [P, DT, 2 * S], F32R), gap("g3", 8),
            ("ob_hl", [P, DT, 2 * S], F32R), gap("g4", 5), ("gate", [P, 2 * DT, S], F32))
        res, _, ple = overlay(("res", [P, DT, S], F32), gap("g5", 95), ("ple", [P, DT, S], F32))
        _, x1_hl = overlay(gap("g6", 16), ("x1_hl", [P, DT, 2 * S], F32R))
        _, act_hl, u, cv, th, sig, av = overlay(
            gap("g7", 48), ("act_hl", [P, FT, 2 * S], F32R), ("u", [P, 2, S + 2], F32),
            ("cv", [P, 2, S], F32), ("th", [P, S], F32), ("sig", [P, S], F32), ("av", [P, S], F32))

        branch_inputs = [(src, dst, k0) for k0 in (0, BLK) for src, dst in ((qa, oa_hl), (qn, ob_hl))]

        bank = [ctx.enter_context(nc.psum_tensor(f"bank{i}", [P, 2 * S], F32)) for i in range(8)]

        def sem(name):
            return ctx.enter_context(nc.semaphore(name))

        loaded = [sem(f"loaded{s}") for s in range(RING)]
        hi_done = sem("hi_done")
        lo_done = sem("lo_done")
        mm_done = sem("mm_done")
        half_done = sem("half_done")
        bank_free = sem("bank_free")
        par_in, kc_in, ke_in, caus_in, dist_in, p_in, res_in = (sem(n) for n in (
            "par_in", "kc_in", "ke_in", "caus_in", "dist_in", "p_in", "res_in"))
        x_in = [sem(f"x_in{c}") for c in range(4)]
        x_hi, x_lo = sem("x_hi"), sem("x_lo")
        pre_mm, pre_read = sem("pre_mm"), sem("pre_read")
        qi_staged, idx_mm, relu_done, idx_used = (sem(n) for n in (
            "qi_staged", "idx_mm", "relu_done", "idx_used"))
        rms_sq, rms_mm, rms_std, rms_n, rms_hi, rms_lo = (sem(n) for n in (
            "rms_sq", "rms_mm", "rms_std", "rms_n", "rms_hi", "rms_lo"))
        rot_mm, rot_read, rot_mul, rot_done = (sem(n) for n in (
            "rot_mm", "rot_read", "rot_mul", "rot_done"))
        q_staged, v_staged, sc_a, sc_b, nmx_ready, exp_done, prob_ready = (sem(n) for n in (
            "q_staged", "v_staged", "sc_a", "sc_b", "nmx_ready", "exp_done", "prob_ready"))
        tr_mm, pt_a, pt_b, pv_mm, o_out, gate_th = (sem(n) for n in (
            "tr_mm", "pt_a", "pt_b", "pv_mm", "o_out", "gate_th"))
        o_hi, o_lo, o_lo_pool, m_lo, p_hi, p_lo = (sem(n) for n in (
            "o_hi", "o_lo", "o_lo_pool", "m_lo", "p_hi", "p_lo"))
        row_added = [sem("row_added"), sem("square_added")]
        res_tile, sq_done, ln_mm, ln_msq, ln_mean, ln_var, ln_std, ln_rstd = (sem(n) for n in (
            "res_tile", "sq_done", "ln_mm", "ln_msq", "ln_mean", "ln_var", "ln_std", "ln_rstd"))
        ln_scaled, ln_pool, out_dve, out_act = (sem(n) for n in ("ln_scaled", "ln_pool", "out_dve", "out_act"))
        x1_hi, x1_lo, x1_kept = (sem(n) for n in ("x1_hi", "x1_lo", "x1_kept"))
        ple_read = sem("ple_read")
        pg_th, pg_sig, cv_done, cv_free, th_done, sig_done, act_lo = (sem(n) for n in (
            "pg_th", "pg_sig", "cv_done", "cv_free", "th_done", "sig_done", "act_lo"))
        pool_step = sem("pool_step")
        dve_step = sem("dve_step")
        out_done = sem("out_done")

        def chunk(g):
            return res[:, GRAN * g:GRAN * g + GRAN]

        def over_tiles(v):
            return v[:].rearrange("p (o s) -> p o s", o=1).to_broadcast([P, GRAN, S])

        def ple_bank(s, k):
            return bank[2 + (2 * s + k) % 6]

        block = ctx.enter_context(nc.Block())

        @block.sync
        def _(sp):
            for what, c in FIRST_LOADS:
                if what == "x":
                    sp.dma_start(x_raw[:, 4 * c:4 * c + 4], x_t[:, 4 * c:4 * c + 4]).then_inc(x_in[c], 16)
                else:
                    sp.dma_start(raw[:, c], stream[c]).then_inc(loaded[c], 16)

            def load_four(i):
                for s in range(RING):
                    sp.wait_ge(lo_done, i * RING + (s - RING + 1))
                    sp.dma_start(raw[:, s], stream[i * RING + s]).then_inc(loaded[s], 16)

            for i in range(1, 4):
                load_four(i)
            sp.dma_start(par[:], params).then_inc(par_in, 16)
            sp.dma_start(kc[:], consts_stay).then_inc(kc_in, 16)
            sp.dma_start(ke[:], consts_early).then_inc(ke_in, 16)
            sp.dma_start(caus[:], masks[0]).then_inc(caus_in, 16)
            sp.dma_start(dist[:], masks[1]).then_inc(dist_in, 16)
            with sp.Fori(4, U_BEFORE_DOWN // RING) as i:
                load_four(i)

            with sp.Fori(0, DT // 2) as i:
                for s in range(2 * U_DOWN_TILE):
                    n = (DOWN_LAST if s % U_DOWN_TILE == U_DOWN_TILE - 1 else BLK) * P
                    sp.wait_ge(lo_done, i * (2 * U_DOWN_TILE) + (U_BEFORE_DOWN + s - RING + 1))
                    sp.dma_start(raw[:, s % RING, 0:n],
                                 stream[i * (2 * U_DOWN_TILE) + (U_BEFORE_DOWN + s), :, 0:n]
                                 ).then_inc(loaded[s % RING], 16)

            for n in range(NG):
                g = n // 2 + n % 2 * len(LN_DVE)
                if g in LN_DVE:
                    sp.wait_ge(out_dve, GRAN * (g + 1))
                else:
                    sp.wait_ge(out_act, GRAN * (g - LN_POOL[0] + 1))
                t = slice(GRAN * g, GRAN * g + GRAN)
                sp.dma_start(out[:, t], res[:, t]).then_inc(out_done, 16)
            sp.wait_ge(out_done, NG * 16)

        @block.tensor
        def _(pe):
            U, T = Count(), Count()
            pe.sem_inc(mm_done, 1)
            pe.sem_inc(idx_mm, 1)
            pe.sem_inc(sc_b, 1)
            pe.sem_inc(pv_mm, 1)

            def block_mm(s, c, b, x, first, last):
                w = slice(c * P, c * P + P)
                pe.matmul(bank[b][:], w_hi[:, s, w], x, start=first, stop=False)
                return pe.matmul(bank[b][:, S:2 * S], w_lo[:, s, w], x[:, 0:S], start=False, stop=last)

            def take_unit():
                pe.wait_ge(lo_done, U.value + 1)

            def take_bank(users=2, ahead=0):
                pe.wait_ge(bank_free, T.value + (3 - users + ahead))

            def unit_of_tile(s, b, x, k0, n=BLK, first=False, last=False, need=None, ahead=0):
                take_unit()
                if first:
                    take_bank(ahead=ahead)
                for c in range(n):
                    if need:
                        need(k0 + c)
                    ins = block_mm(s, c, b, x[:, k0 + c], first and c == 0, last and c == n - 1)
                ins.then_inc(mm_done, 1)
                U.add()
                if last:
                    T.add()

            def two_tiles(xs, before=None, needs=(None, None)):
                def body(i):
                    for s in range(4):
                        if before and s % 2 == 0:
                            before(i)
                        unit_of_tile(s, s // 2, xs[s // 2], BLK * (s % 2), first=s % 2 == 0,
                                     last=s % 2 == 1, need=needs[s // 2])
                return body

            def by_turns(xs, needs):
                def body(i):
                    for s in range(4):
                        unit_of_tile(s, s % 2, xs[s % 2], BLK * (s // 2), first=s < 2, last=s >= 2,
                                     need=needs[s % 2], ahead=s % 2)
                return body

            def each(sem_, n):
                def need(k):
                    if k % n == 0:
                        pe.wait_ge(sem_, k // n + 1)
                return need

            def outputs(n):
                def need(k):
                    if k % 2 == 0 and n == 1 and k >= BLK:
                        pe.wait_ge(o_lo_pool, (k - BLK) // 2 + 1)
                    elif k % 2 == 0:
                        pe.wait_ge(o_lo, k // 2 + 1 + 4 * (k // BLK) + 4 * n)
                return need

            STD = ((U, 4), (T, 2))
            x2 = (x_hl, x_hl)

            def tiles_split(sem_, start=0):
                def need(k):
                    if DT - 4 <= k < DT:
                        pe.wait_ge(sem_, k + 1 + start)
                    elif k % 4 == 0:
                        pe.wait_ge(sem_, k + 4 + start)
                return need

            def tiles_of_unit(x, k0, nk, per, after=None):
                def body(i):
                    for s in range(4):
                        take_unit()
                        for t in range(per):
                            b = (2 + s * per + t) % 4
                            take_bank(4)
                            for k in range(nk):
                                ins = block_mm(s, t * nk + k, b, x[:, k0 + k], k == 0, k == nk - 1)
                            T.add()
                        ins.then_inc(mm_done, 1)
                        U.add()
                        if after:
                            after(i, s)
                return body

            two_tiles(x2, needs=(each(x_lo, 4), None))(0)
            repeat(pe, N_FEAT // 2 - 1, two_tiles(x2), *STD)

            pe.wait_ge(kc_in, 16)
            pe.wait_ge(ke_in, 16)
            pe.wait_ge(bank_free, 2 + 4)
            for n, t in enumerate((T_WIDX, T_VA)):
                for tb in range(2):
                    pe.transpose(bank[6][:, (2 * n + tb) * P:(2 * n + tb + 1) * P],
                                 feat[:, t, tb * P:tb * P + P], ident)
            pe.matmul(bank[7][:, 0:S], ke[:, K_DUP:K_DUP + P], feat[:, T_KIDX], start=True, stop=True)
            pe.matmul(bank[7][:, S:2 * S], ke[:, K_DUPROT:K_DUPROT + P], feat[:, T_KIDX],
                      start=True, stop=True).then_inc(pre_mm, 1)

            J = Count()

            def indexer(i):
                pe.wait_ge(qi_staged, J.value + 1)
                pe.wait_ge(relu_done, 2 * J.value + 2)
                for q, c0, nk in BLOCKS:
                    for b in range(2):
                        h = slice(ROPE * b, ROPE * b + ROPE)
                        key = feat[h, T_KIDX if b == 0 else T_WIDX]
                        ins = pe.matmul(bank[4 + b][:, c0:c0 + nk], qi_st[h, q * P:q * P + P],
                                        key[:, 0:nk], start=True, stop=True)
                ins.then_inc(idx_mm, 1)
                J.add()

            pe.wait_ge(bank_free, 2 + 12)
            repeat(pe, 4, two_tiles(x2, indexer), *STD, (J, 2))
            pe.wait_ge(pre_read, 1)
            for n in range(2):
                pe.wait_ge(rms_sq, n + 1)
                for t in range(LT):
                    ins = pe.matmul(bank[6 + n][:, 0:S], mean_of, c_sq[:, n, t], start=t == 0, stop=t == LT - 1)
                ins.then_inc(rms_mm, 1)
            repeat(pe, 4, two_tiles(x2), *STD)

            pe.wait_ge(rms_lo, 1)
            repeat(pe, U_UQ // 4, tiles_of_unit(c_hl, 0, LT, 2), (U, 4), (T, 8))
            pe.wait_ge(rms_lo, 2)
            J = Count()

            def rotate(i, s):
                pe.wait_ge(rot_done, J.value + 1)
                pe.matmul(bank[4 + s % 2][:, 0:S], ke[:, K_ROT:K_ROT + P],
                          qp[:, i * 4 + s], start=True, stop=True).then_inc(rot_mm, 1)
                J.add()

            repeat(pe, U_UK // 4, tiles_of_unit(c_hl, LT, LT, 2, rotate), (U, 4), (T, 8), (J, 4))

            def values(i):
                for s in range(4):
                    take_unit()
                    take_bank()
                    for tb in range(2):
                        o = bank[s % 2][:, tb * S:tb * S + S]
                        for k in range(LT):
                            c_hi = c_hl[:, LT + k, tb * P:tb * P + P]
                            c_lo = c_hl[:, LT + k, S + tb * P:S + tb * P + P]
                            w = slice(k * S, k * S + S)
                            pe.matmul(o, c_hi, w_hi[:, s, w], start=k == 0, stop=False)
                            pe.matmul(o, c_hi, w_lo[:, s, w], start=False, stop=False)
                            ins = pe.matmul(o, c_lo, w_hi[:, s, w], start=False, stop=k == LT - 1)
                    ins.then_inc(mm_done, 1)
                    U.add()
                    T.add()

            repeat(pe, U_UV // 4, values, (U, 4), (T, 4))

            Hd = Count()

            def heads(i):
                for par_ in range(2):
                    half_ = slice(ROPE * par_, ROPE * par_ + ROPE)
                    h = Hd.value
                    pe.wait_ge(q_staged, h + 1)
                    for q, c0, nk in BLOCKS:
                        ins = pe.matmul(bank[2][:, c0:c0 + nk], qa_st[:, q * P:q * P + P], ka_s[:, 0:nk],
                                        start=True, stop=True)
                    ins.then_inc(sc_a, 1)
                    for q, c0, nk in BLOCKS:
                        pe.matmul(bank[3][:, c0:c0 + nk], qn_st[:, q * P:q * P + P],
                                  kn[:, i * 2 + par_, 0:nk], start=True, stop=False)
                        ins = pe.matmul(bank[3][:, c0:c0 + nk], qp_st[half_, q * P:q * P + P],
                                        kpe[half_, 0:nk], start=False, stop=True)
                    ins.then_inc(sc_b, 1)
                    unit_of_tile(0, 0, x_hl, 0, first=True)
                    unit_of_tile(1, 0, x_hl, BLK, last=True)
                    unit_of_tile(2, 1, x_hl, 0, first=True)
                    pe.wait_ge(prob_ready, 4 * h + 4)
                    for m in range(2):
                        for c in range(3):
                            ins = pe.transpose(bank[4 + m][:, c * P:c * P + P], prob[:, m, c * P:c * P + P], ident)
                    ins.then_inc(tr_mm, 1)
                    unit_of_tile(3, 1, x_hl, BLK, last=True)
                    pe.wait_ge(pt_a, h + 1)
                    pe.wait_ge(pt_b, h + 1)
                    pe.wait_ge(v_staged, h + 1)
                    pe.wait_ge(o_out, h + 1)
                    for m, v in enumerate((va, v_st)):
                        pe.matmul(bank[6 + par_][:, m * S:m * S + S], v[:, 0], prob_t[:, m, 0:S],
                                  start=True, stop=False)
                        ins = pe.matmul(bank[6 + par_][:, m * S + P:m * S + S], v[:, 1], prob_t[:, m, S:SC],
                                        start=False, stop=True)
                    ins.then_inc(pv_mm, 1)
                    Hd.add()

            pe.wait_ge(pre_read, 2)
            repeat(pe, HEADS // 2, heads, (U, 8), (T, 4), (Hd, 2))

            repeat(pe, DT, by_turns((oa_hl, ob_hl), needs=(outputs(0), outputs(1))), *STD)

            def norm_sums(w):
                for n in range(2):
                    pe.wait_ge(bank_free, T.value + 1 + n)
                    pe.wait_ge(row_added[n], (DT - 1) * (w + 1) + 2)
                    pe.matmul(bank[n][:, 0:S], mean_of, rows[:, n], start=True, stop=False)
                for n, (done, last) in enumerate(((res_tile, res[:, DT - 1]), (sq_done, sq[:, 1]))):
                    pe.wait_ge(done, DT * (w + 1))
                    pe.matmul(bank[n][:, 0:S], mean_of, last, start=False, stop=True).then_inc(ln_mm, 1)

            def embedding_unit(s):
                take_unit()
                for t in range(4):
                    o = ple_bank(s, t // 2)[:, t % 2 * S:t % 2 * S + S]
                    for k in range(2):
                        w = slice((t * 2 + k) * P, (t * 2 + k + 1) * P)
                        pe.matmul(o, w_hi[:, s, w], p_hl[:, k, 0:S], start=k == 0, stop=False)
                        pe.matmul(o, w_hi[:, s, w], p_hl[:, k, S:2 * S], start=False, stop=False)
                        ins = pe.matmul(o, w_lo[:, s, w], p_hl[:, k, 0:S], start=False, stop=k == 1)
                ins.then_inc(mm_done, 1)
                U.add()

            repeat(pe, DT // 2, by_turns((m_hl, m_hl), needs=(tiles_split(m_lo), None)), *STD)
            pe.wait_ge(p_lo, 1)
            embedding_unit(0)
            norm_sums(0)
            embedding_unit(1)
            embedding_unit(2)
            pe.wait_ge(ple_read, 2)
            embedding_unit(3)

            repeat(pe, DT // 2, by_turns((x1_hl, x1_hl), needs=(each(x1_lo, GRAN), None)), *STD)
            repeat(pe, FT, two_tiles((x1_hl, x1_hl)), *STD)

            def down(i):
                for s in range(2 * U_DOWN_TILE):
                    t, c = divmod(s, U_DOWN_TILE)
                    lastu = c == U_DOWN_TILE - 1
                    unit_of_tile(s % RING, t, act_hl, c * BLK, DOWN_LAST if lastu else BLK,
                                 first=c == 0, last=lastu, need=tiles_split(act_lo, 1) if t == 0 else None)

            repeat(pe, DT // 2, down, (U, 2 * U_DOWN_TILE), (T, 2))
            norm_sums(1)

        @block.scalar
        def _(act):
            U, T = Count(), Count()
            act.sem_inc(relu_done, 2)
            act.sem_inc(gate_th, 2)

            def split_hi(s, n=UNIT):
                v, turn = (s + AHEAD) % RING, (s + AHEAD) // RING
                act.wait_ge(loaded[v], (U.value - s) * (16 // RING) + 16 * (turn + 1))
                act.wait_ge(mm_done, U.value + 1)
                act.activation(w_hi[:, v, 0:n], raw[:, v, 0:n], ACT.Copy).then_inc(hi_done, 1)

            def read_half(b, scale=1.0):
                act.wait_ge(mm_done, U.value + 1)
                act.wait_ge(bank_free, T.value + 1)
                act.activation(half[:, b % 2], bank[b][:, 0:S], ACT.Copy, scale=scale).then_inc(half_done, 1)
                T.add()

            def two_tiles(scale=1.0, before=None, after=None, ends=(1, 3)):
                def body(i):
                    for s in range(4):
                        split_hi(s)
                        U.add()
                        if s % 2 and before:
                            before(i)
                        if s in ends:
                            read_half(ends.index(s), scale)
                            if after:
                                after(i, ends.index(s))
                return body

            def tiles_of_unit(per, after=None):
                def body(i):
                    for s in range(4):
                        split_hi(s)
                        U.add()
                        for t in range(per):
                            read_half((2 + s * per + t) % 4)
                        if after:
                            after(s)
                return body

            STD = ((U, 4), (T, 2))

            for what, c in FIRST_LOADS[:-1]:
                if what == "x":
                    act.wait_ge(x_in[c], 16)
                    act.activation(x_hl[:, 4 * c:4 * c + 4, 0:S], x_raw[:, 4 * c:4 * c + 4], ACT.Copy
                                   ).then_inc(x_hi, 1)
                else:
                    act.wait_ge(loaded[c], 16)
                    act.activation(w_hi[:, c], raw[:, c], ACT.Copy).then_inc(hi_done, 1)

            repeat(act, N_FEAT // 2, two_tiles(), *STD)
            for n, t in enumerate((T_CQ, T_CKV)):
                act.wait_ge(bank_free, 2 + N_FEAT)
                act.activation(c_sq[:, n], feat[:, t:t + LT], ACT.Square).then_inc(rms_sq, 1)

            J = Count()

            def indexer(i):
                act.wait_ge(idx_mm, J.value + 2)
                for b in range(2):
                    act.wait_ge(idx_used, 2 * J.value + 1 + b)
                    act.activation(rel[:, b], bank[4 + b][:, 0:SC], ACT.Relu).then_inc(relu_done, 1)
                J.add()

            repeat(act, 4, two_tiles(before=indexer), *STD, (J, 2))
            act.wait_ge(par_in, 16)
            for n in range(2):
                act.wait_ge(rms_mm, n + 1)
                k = SCALE_B ** 2 if n == 0 else 1.0
                e = C_EPS + (2 if n == 0 else 1)
                act.activation(c_std[:, n], bank[6 + n][:, 0:S], ACT.Sqrt, scale=D / (LORA * k),
                               bias=par[:, e:e + 1]).then_inc(rms_std, 1)
            for n, t in enumerate((T_CQ, T_CKV)):
                act.wait_ge(rms_n, LT * (n + 1))
                act.activation(c_hl[:, LT * n:LT * n + LT, 0:S], feat[:, t:t + LT], ACT.Copy
                               ).then_inc(rms_hi, 1)
                repeat(act, 2, two_tiles(), *STD)

            R = Count()

            def read_rotation(s):
                act.wait_ge(rot_mm, R.value + 1)
                act.wait_ge(rot_done, R.value + 1)
                act.activation(tmp[:, s % 2], bank[4 + s % 2][:, 0:S], ACT.Copy).then_inc(rot_read, 1)
                R.add()

            repeat(act, U_UQ // 4, tiles_of_unit(2), (U, 4), (T, 8))
            repeat(act, U_UK // 4, tiles_of_unit(2, after=read_rotation), (U, 4), (T, 8), (R, 4))

            def values(i):
                for s in range(4):
                    split_hi(s)
                    U.add()
                    act.wait_ge(mm_done, U.value + 1)
                    act.activation(v_mla[:, :, bass.ds(i * (4 * S) + s * S, S)],
                                   bank[s % 2][:].rearrange("p (b n) -> p b n", b=2), ACT.Copy
                                   ).then_inc(bank_free, 1)
                    T.add()

            act.wait_ge(bank_free, T.value + 2)
            repeat(act, U_UV // 4, values, (U, 4), (T, 4))

            Hd = Count()

            def heads(i):
                for par_ in range(2):
                    h = Hd.value
                    split_hi(0)
                    U.add()
                    split_hi(1)
                    U.add()
                    act.wait_ge(nmx_ready, 2 * h + 2)
                    for m in range(2):
                        for q, c0, nk in BLOCKS:
                            c = 2 * m + q
                            act.activation(prob[:, m, c0:c0 + nk], prob[:, m, c0:c0 + nk], ACT.Exp,
                                           bias=nmx[:, m, q:q + 1], accum_out=sm[:, c:c + 1]).then_inc(exp_done, 1)
                    read_half(0)
                    split_hi(2)
                    U.add()
                    act.wait_ge(bank_free, T.value + 2)
                    act.activation(gate[:, i * 4 + 2 * par_], tmp[:, 0], ACT.Tanh, scale=0.5).then_inc(gate_th, 1)
                    split_hi(3)
                    U.add()
                    act.wait_ge(tr_mm, h + 1)
                    act.wait_ge(pv_mm, h + 1)
                    act.activation(prob_t[:, 0], bank[4][:, 0:SC], ACT.Copy).then_inc(pt_a, 1)
                    read_half(1)
                    act.wait_ge(bank_free, T.value + 2)
                    act.activation(gate[:, i * 4 + 2 * par_ + 1], tmp[:, 1], ACT.Tanh, scale=0.5
                                   ).then_inc(gate_th, 1)
                    Hd.add()

            repeat(act, HEADS // 2, heads, (U, 8), (T, 4), (Hd, 2))

            act.wait_ge(mm_done, U.value + 1)
            for src, dst, k0 in branch_inputs:
                for k in range(k0, k0 + BLK, 2):
                    act.wait_ge(o_out, 2 + k + 2)
                    act.activation(dst[:, k:k + 2, 0:S], src[:, k:k + 2], ACT.Copy).then_inc(o_hi, 1)
                if dst is ob_hl and k0 == 0:
                    act.wait_ge(pv_mm, HEADS + 1)
                    act.dma_start(p_raw[:], p_t).then_inc(p_in, 16)
            act.wait_ge(p_in, 16)
            act.activation(p_hl[:, :, 0:S], p_raw[:], ACT.Copy).then_inc(p_hi, 1)
            repeat(act, DT, two_tiles(0.5, ends=TURNS), *STD)
            act.dma_start(res[:], x_t).then_inc(res_in, 16)

            N, A = Count(), Count()

            def squares(i, b):
                act.wait_ge(res_tile, N.value + 1)
                act.wait_ge(row_added[1], A.value + 1)
                A.add()
                act.activation(sq[:, b], res[:, i * 2 + b], ACT.Square).then_inc(sq_done, 1)
                N.add()

            def bring_sqrt_table():
                act.activation(eps_std[:], par[:, C_EPS:C_EPS + 1], ACT.Sqrt)

            def norm(w):
                act.wait_ge(ln_mean, w + 1)
                act.activation(var[:], mean[:], ACT.Square).then_inc(ln_msq, 1)
                act.wait_ge(ln_var, w + 1)
                act.activation(rstd[:], rstd[:], ACT.Sqrt, bias=par[:, C_EPS:C_EPS + 1]).then_inc(ln_std, 1)

            repeat(act, DT // 2 - 1, two_tiles(after=squares, ends=TURNS), *STD, (N, 2), (A, 2))
            bring_sqrt_table()
            two_tiles(after=squares, ends=TURNS)(DT // 2 - 1)
            A.base = A.base - 1

            def next_unit(s):
                split_hi(s)
                U.add()

            def keep_embedding(s):
                act.wait_ge(mm_done, first_ple + s + 2)
                for k in range(2):
                    act.activation(ple[:, 4 * s + 2 * k:4 * s + 2 * k + 2],
                                   ple_bank(s, k)[:].rearrange("p (t s) -> p t s", t=2), ACT.Copy
                                   ).then_inc(ple_read, 1)

            def x1_high(g):
                if g in LN_DVE:
                    act.wait_ge(ln_scaled, g + 1)
                    for t in range(GRAN * g, GRAN * g + GRAN):
                        act.activation(x1_hl[:, t, 0:S], res[:, t], ACT.Identity,
                                       bias=par[:, C_LN1B + t:C_LN1B + t + 1]).then_inc(x1_hi, 1)
                else:
                    act.wait_ge(ln_pool, g - LN_POOL[0] + 1)
                    t = slice(GRAN * g, GRAN * g + GRAN)
                    act.activation(x1_hl[:, t, 0:S], res[:, t], ACT.Copy).then_inc(x1_hi, GRAN)

            first_ple = U.value
            next_unit(0)
            norm(0)
            next_unit(1)
            keep_embedding(0)
            x1_high(0)
            next_unit(2)
            x1_high(1)
            x1_high(2)
            x1_high(3)
            next_unit(3)
            for g in LN_POOL:
                x1_high(g)
            keep_embedding(1)
            keep_embedding(2)
            keep_embedding(3)

            G = Count()

            def pg_sigmoid(i, b):
                if b == 0:
                    return
                for b in range(2):
                    act.wait_ge(bank_free, T.value + 1 + b)
                    act.activation(tmp[:, b], tmp[:, b], ACT.Tanh, scale=0.5,
                                   bias=par[:, bass.ds(i * 2 + (C_BPG + b), 1)]).then_inc(pg_th, 1)
                for b in range(2):
                    act.wait_ge(pg_th, G.value + 1)
                    act.activation(tmp[:, b], tmp[:, b], ACT.Copy, scale=0.5, bias=0.5).then_inc(pg_sig, 1)
                    G.add()

            repeat(act, DT // 2, two_tiles(after=pg_sigmoid, ends=TURNS), *STD, (G, 2))

            J = Count()

            def silu_tanh(i, b):
                if b == 1:
                    act.wait_ge(cv_done, 2 * J.value + 1)
                    act.wait_ge(cv_free, J.value + 1)
                    act.activation(th[:], cv[:, 0], ACT.Tanh, scale=0.5).then_inc(th_done, 1)
                    act.wait_ge(th_done, J.value + 1)
                    act.activation(sig[:], th[:], ACT.Copy, bias=0.5, scale=0.5).then_inc(sig_done, 1)
                    J.add()

            repeat(act, FT, two_tiles(after=silu_tanh), *STD, (J, 1))

            def down(final):
                def body(i):
                    n_s = 2 * U_DOWN_TILE
                    for s in range(n_s):
                        if not (final and s + AHEAD >= n_s):
                            split_hi_down(s)
                        U.add()
                        if s % U_DOWN_TILE == U_DOWN_TILE - 1:
                            read_half(s // U_DOWN_TILE)
                            squares(i, s // U_DOWN_TILE)
                return body

            def split_hi_down(s):
                n = DOWN_LAST if (s + AHEAD) % U_DOWN_TILE == U_DOWN_TILE - 1 else BLK
                v, turn = (s + AHEAD) % RING, (s + AHEAD) // RING
                act.wait_ge(loaded[v], (U.value - s) * (16 // RING) + 16 * (turn + 1))
                act.wait_ge(mm_done, U.value + 1)
                act.activation(w_hi[:, v, 0:n * P], raw[:, v, 0:n * P], ACT.Copy).then_inc(hi_done, 1)

            repeat(act, DT // 2 - 1, down(False), (U, 2 * U_DOWN_TILE), (T, 2), (N, 2), (A, 2))
            bring_sqrt_table()
            down(True)(DT // 2 - 1)
            norm(1)
            for g in LN_POOL:
                act.wait_ge(ln_pool, len(LN_POOL) + g - LN_POOL[0] + 1)
                for t in range(GRAN * g, GRAN * g + GRAN):
                    act.activation(res[:, t], res[:, t], ACT.Identity, scale=par[:, C_LN2G + t:C_LN2G + t + 1],
                                   bias=par[:, C_LN2B + t:C_LN2B + t + 1]).then_inc(out_act, 1)

        @block.vector
        def _(dve):
            U, T, H, V = Count(), Count(), Count(), Count()
            dve.sem_inc(bank_free, 2)
            dve.sem_inc(idx_used, 2)
            dve.sem_inc(rot_done, 2)
            dve.sem_inc(o_out, 2)

            def step(ins):
                ins.then_inc(dve_step, 1)
                V.add()

            def steps_done():
                dve.wait_ge(dve_step, V.value)

            def sub(o, a, b):
                return dve.tensor_tensor(o, a, b, ALU.subtract)

            def stt(o, a, s, b, op0, op1):
                return dve.scalar_tensor_tensor(out=o, in0=a, scalar=s, in1=b, op0=op0, op1=op1)

            def f32(ap):
                return ap.bitcast(F32)

            def split_lo(s, n=UNIT):
                v = (s + AHEAD) % RING
                dve.wait_ge(hi_done, U.value + (AHEAD + 1))
                sub(w_lo[:, v, 0:n], raw[:, v, 0:n], f32(w_hi[:, v, 0:n])).then_inc(lo_done, 1)

            def add_half(b, o, scale=1.0):
                dve.wait_ge(half_done, H.value + 1)
                stt(o, bank[b][:, S:2 * S], scale, half[:, b % 2], ALU.mult, ALU.add).then_inc(bank_free, 1)
                H.add()
                T.add()

            def tile_done():
                dve.wait_ge(bank_free, T.value + 2)

            def two_tiles(take, ends=(1, 3)):
                def body(i):
                    for s in range(4):
                        split_lo(s)
                        U.add()
                        if s in ends:
                            take(i, ends.index(s))
                return body

            STD = ((U, 4), (T, 2), (H, 2))

            step(dve.memset(score[:], 0.0))
            for what, c in FIRST_LOADS[:-1]:
                if what == "x":
                    dve.wait_ge(x_hi, c + 1)
                    t = slice(4 * c, 4 * c + 4)
                    sub(x_hl[:, t, S:2 * S], x_raw[:, t], f32(x_hl[:, t, 0:S])).then_inc(x_lo, 1)
                else:
                    dve.wait_ge(hi_done, c + 1)
                    sub(w_lo[:, c], raw[:, c], f32(w_hi[:, c])).then_inc(lo_done, 1)

            repeat(dve, N_FEAT // 2, two_tiles(lambda i, b: add_half(b, feat[:, i * 2 + b])), *STD)

            dve.wait_ge(pre_mm, 1)
            dve.wait_ge(ke_in, 16)
            for tb in range(2):
                step(dve.tensor_copy(wix[:, tb], bank[6][:, tb * P:tb * P + HEADS]))
                step(dve.tensor_copy(va[:, tb], bank[6][:, S + tb * P:S + tb * P + P]))
            step(dve.tensor_tensor(kpe[:], bank[7][:, 0:S], ke[:, K_COS:K_COS + S], ALU.mult))
            step(dve.tensor_tensor(tmp[:, 0], bank[7][:, S:2 * S], ke[:, K_SIN:K_SIN + S], ALU.mult))
            dve.wait_ge(bank_free, 2 + 4)
            step(dve.tensor_scalar(ka_s[:], feat[:, T_KA], SCALE_A, None, ALU.mult))
            steps_done()
            dve.sem_inc(pre_read, 1)
            step(dve.tensor_tensor(kpe[:], kpe[:], tmp[:, 0], ALU.add))
            steps_done()
            dve.sem_inc(pre_read, 1)

            J = Count()

            def q_and_indexer(i, b):
                add_half(b, qa[:, i * 2 + b])
                for e in range(2):
                    dve.wait_ge(relu_done, 2 * J.value + 3 + e)
                    dve.wait_ge(idx_used, 2 * J.value + 2 + e)
                    for q, c0, nk in BLOCKS:
                        ins = stt(score[:, c0:c0 + nk], rel[:, e, c0:c0 + nk],
                                  wix[:, q, bass.ds(i * 4 + (2 * b + e), 1)],
                                  score[:, c0:c0 + nk], ALU.mult, ALU.add)
                    ins.then_inc(idx_used, 1)
                J.add()

            repeat(dve, 4, two_tiles(q_and_indexer), *STD, (J, 2))
            dve.wait_ge(par_in, 16)

            def latent_norm(n):
                t = (T_CQ, T_CKV)[n]
                dve.wait_ge(rms_std, n + 1)
                step(dve.reciprocal(c_std[:, n], c_std[:, n]))
                steps_done()
                for k in range(LT):
                    g = (C_QN, C_KVN)[n] + k
                    stt(feat[:, t + k], feat[:, t + k], par[:, g:g + 1], c_std[:, n], ALU.mult, ALU.mult
                        ).then_inc(rms_n, 1)

            def latent_split(n):
                t, k = (T_CQ, T_CKV)[n], slice(LT * n, LT * n + LT)
                dve.wait_ge(rms_hi, n + 1)
                sub(c_hl[:, k, S:2 * S], feat[:, t:t + LT], f32(c_hl[:, k, 0:S])).then_inc(rms_lo, 1)

            latent_norm(0)
            step(dve.tensor_scalar(par[:, C_BPG:C_BPG + DT], par[:, C_BPG:C_BPG + DT], 0.5, None, ALU.mult))

            dve.wait_ge(caus_in, 16)
            dve.wait_ge(idx_used, 2 + HEADS)
            step(dve.tensor_tensor(score[:], score[:], caus[:], ALU.add))
            steps_done()
            step(dve.tensor_copy(work[:], score[:]))

            def topk_round():
                for q, c0, nk in BLOCKS:
                    steps_done()
                    dve.memset(spare[:], 0.0)
                    step(dve.max(top8[:, q], work[:, c0:c0 + nk]))
                    steps_done()
                    dve.memset(spare[:], 0.0)
                    step(dve.match_replace(out=work[:, c0:c0 + nk], in_to_replace=top8[:, q],
                                           in_values=work[:, c0:c0 + nk], imm_value=-3e38))

            def q_and_topk(first):
                def take(i, b):
                    add_half(b, qa[:, i * 2 + (DT // 2 + 2 * first + b)])
                    topk_round()
                return take

            two_tiles(q_and_topk(0))(0)
            latent_norm(1)
            two_tiles(q_and_topk(1))(0)
            latent_split(0)
            two_tiles(q_and_topk(2))(0)
            latent_split(1)
            two_tiles(q_and_topk(3))(0)
            gt, eq = rel[:, 0], rel[:, 1]

            def select(part):
                steps_done()
                if part == 0:
                    for q, c0, nk in BLOCKS:
                        c = slice(c0, c0 + nk)
                        step(dve.tensor_scalar(gt[:, c], score[:, c], top8[:, q, 7:8], None, ALU.is_gt))
                        step(dve.tensor_scalar(eq[:, c], score[:, c], top8[:, q, 7:8], None, ALU.is_equal))
                elif part == 1:
                    for q, c0, nk in BLOCKS:
                        c = slice(c0, c0 + nk)
                        step(dve.tensor_reduce(cnt[:, q:q + 1], gt[:, c], AX_X, ALU.add))
                        step(dve.tensor_tensor_scan(work[:, c], eq[:, c], eq[:, c], 0.0, ALU.add, ALU.max))
                elif part == 2:
                    step(dve.tensor_scalar(cnt[:], cnt[:], -1.0, float(TOPK), ALU.mult, ALU.add))
                    steps_done()
                    for q, c0, nk in BLOCKS:
                        c = slice(c0, c0 + nk)
                        step(stt(work[:, c], work[:, c], cnt[:, q:q + 1], eq[:, c], ALU.is_le, ALU.mult))
                else:
                    step(dve.tensor_tensor(work[:], work[:], gt, ALU.add))
                    steps_done()
                    step(dve.tensor_scalar(work[:], work[:], -1.0, -NEG, ALU.add, ALU.mult))
                    steps_done()
                    step(dve.tensor_tensor(madd[:], work[:], caus[:], ALU.add))

            R = Count()

            def rope_sum(j, b):
                dve.wait_ge(rot_mul, 2 * R.value + 2)
                dve.tensor_tensor(qp[:, j], qp[:, j], tmp[:, b], ALU.add).then_inc(rot_done, 1)
                R.add()

            def latent_tiles(base, rope, between=None):
                def body(i):
                    for s in range(4):
                        split_lo(s)
                        U.add()
                        if rope and s:
                            rope_sum(i * 4 + (s - 1), (s - 1) % 2)
                        for t in range(2):
                            add_half((2 * s + t + 2) % 4, qk[:, i * 8 + (base + 2 * s + t)])
                        if between:
                            between(s)
                    if rope:
                        rope_sum(i * 4 + 3, 1)
                return body

            latent_tiles(0, False, select)(0)
            steps_done()
            repeat(dve, U_UQ // 4 - 1, latent_tiles(8, False), (U, 4), (T, 8), (H, 8))
            repeat(dve, U_UK // 4, latent_tiles(24, True), (U, 4), (T, 8), (H, 8), (R, 4))

            def values(i):
                for s in range(4):
                    split_lo(s)
                    U.add()
                    T.add()

            repeat(dve, U_UV // 4, values, (U, 4), (T, 4))

            Hd = Count()
            dve.wait_ge(dist_in, 16)

            def gate_tile(b):
                dve.wait_ge(gate_th, G.value + 1)
                add_half(b, tmp[:, b])
                G.add()

            G = Count()

            def heads(i):
                for par_ in range(2):
                    h = Hd.value
                    split_lo(0)
                    U.add()
                    step(stt(bias[:], dist[:], par[:, bass.ds(i * 2 + (C_SLOPE + par_), 1)], madd[:],
                             ALU.mult, ALU.add))
                    steps_done()
                    dve.wait_ge(sc_a, h + 1)
                    step(dve.tensor_tensor(prob[:, 0], bank[2][:, 0:SC], bias[:], ALU.add))
                    dve.wait_ge(sc_b, h + 2)
                    step(dve.tensor_tensor(prob[:, 1], bank[3][:, 0:SC], caus[:], ALU.add))
                    steps_done()
                    for q, c0, nk in BLOCKS:
                        dve.tensor_reduce(nmx[:, :, q], prob[:, :, c0:c0 + nk], AX_X, ALU.max, negate=True
                                          ).then_inc(nmx_ready, 1)
                    split_lo(1)
                    U.add()
                    dve.wait_ge(exp_done, 4 * h + 4)
                    step(dve.reciprocal(rsm[:], sm[:]))
                    steps_done()
                    for m in range(2):
                        for q, c0, nk in BLOCKS:
                            c = 2 * m + q
                            dve.tensor_scalar(prob[:, m, c0:c0 + nk], prob[:, m, c0:c0 + nk],
                                              rsm[:, c:c + 1], None, ALU.mult).then_inc(prob_ready, 1)
                    gate_tile(0)
                    split_lo(2)
                    U.add()
                    dve.wait_ge(tr_mm, h + 1)
                    dve.wait_ge(pv_mm, h + 1)
                    dve.tensor_copy(prob_t[:, 1], bank[5][:, 0:SC]).then_inc(pt_b, 1)
                    split_lo(3)
                    U.add()
                    gate_tile(1)
                    dve.wait_ge(pv_mm, h + 2)
                    step(dve.tensor_scalar(qa[:, i * 2 + par_], bank[6 + par_][:, 0:S], 1.0, None, ALU.mult))
                    steps_done()
                    dve.tensor_scalar(qn[:, i * 2 + par_], bank[6 + par_][:, S:2 * S], 1.0, None, ALU.mult
                                      ).then_inc(o_out, 1)
                    Hd.add()

            repeat(dve, HEADS // 2, heads, (U, 8), (T, 4), (H, 4), (Hd, 2), (G, 4), (V, 10))

            n = 0
            dve.wait_ge(o_out, HEADS + 2)
            for src, dst, k0 in branch_inputs[0:3]:
                for k in range(k0, k0 + BLK, 2):
                    n += 1
                    dve.wait_ge(o_hi, n)
                    sub(dst[:, k:k + 2, S:2 * S], src[:, k:k + 2], f32(dst[:, k:k + 2, 0:S])).then_inc(o_lo, 1)
            dve.wait_ge(gate_th, 2 + 2 * DT)

            def split_tile(hl, j, v, done):
                step(dve.tensor_scalar(hl[:, j, 0:S], v, 1.0, None, ALU.mult))
                steps_done()
                sub(hl[:, j, S:2 * S], v, f32(hl[:, j, 0:S])).then_inc(done, 1)

            def gated(i, b):
                add_half(b, tmp[:, b], 0.5)
                tile_done()
                step(stt(tmp[:, b], gate[:, i * 2 + b], 1.0, tmp[:, b], ALU.add, ALU.mult))
                if b:
                    steps_done()
                    step(dve.tensor_tensor(merged[:], tmp[:, 0], tmp[:, 1], ALU.add))
                    steps_done()
                    split_tile(m_hl, i, merged[:], m_lo)

            repeat(dve, DT, two_tiles(gated, TURNS), *STD, (V, 4))

            dve.wait_ge(m_lo, DT)

            def norm(w):
                dve.wait_ge(ln_mm, 2 * w + 1)
                dve.tensor_copy(mean[:], bank[0][:, 0:S]).then_inc(ln_mean, 1)
                dve.wait_ge(ln_msq, w + 1)
                dve.wait_ge(ln_mm, 2 * w + 2)
                step(dve.tensor_tensor(var[:], bank[1][:, 0:S], var[:], ALU.subtract))
                steps_done()
                dve.tensor_scalar(rstd[:], var[:], 0.0, None, ALU.max).then_inc(ln_var, 1)
                dve.wait_ge(ln_mean, w + 1)
                centre(0)
                dve.wait_ge(ln_std, w + 1)
                step(dve.reciprocal(rstd[:], rstd[:]))
                steps_done()
                dve.sem_inc(ln_rstd, 1)

            def centre(g):
                step(sub(chunk(g), chunk(g), over_tiles(mean)))

            def scale(g, c_g, done=None):
                steps_done()
                for t in range(GRAN * g, GRAN * g + GRAN):
                    step(stt(res[:, t], res[:, t], par[:, c_g + t:c_g + t + 1], rstd[:], ALU.mult, ALU.mult))
                steps_done()
                if done:
                    dve.sem_inc(done, 1)
                if g + 1 in LN_DVE:
                    centre(g + 1)

            def x1_split(g):
                dve.wait_ge(x1_hi, GRAN * (g + 1))
                if g in LN_DVE:
                    for t in range(GRAN * g, GRAN * g + GRAN):
                        ins = stt(x1_hl[:, t, S:2 * S], res[:, t], par[:, C_LN1B + t:C_LN1B + t + 1],
                                  f32(x1_hl[:, t, 0:S]), ALU.add, ALU.subtract)
                else:
                    t = slice(GRAN * g, GRAN * g + GRAN)
                    ins = sub(x1_hl[:, t, S:2 * S], res[:, t], f32(x1_hl[:, t, 0:S]))
                ins.then_inc(x1_lo, 1)

            def next_unit(s):
                split_lo(s)
                U.add()

            def residual(i, b):
                add_half(b, tmp[:, b])
                t = i * 2 + b
                tile_done()
                dve.wait_ge(res_in, 16)
                stt(res[:, t], res[:, t], ALPHA, tmp[:, b], ALU.mult, ALU.add).then_inc(res_tile, 1)

            repeat(dve, DT // 2, two_tiles(residual, TURNS), *STD)
            norm(0)
            for g in range(NG):
                if g in LN_DVE:
                    scale(g, C_LN1G, ln_scaled)
                if 1 <= g <= 4:
                    next_unit(g - 1)
                if g:
                    x1_split(g - 1)
            x1_split(NG - 1)
            dve.wait_ge(ple_read, 8)
            dve.wait_ge(x1_kept, 1)

            G = Count()

            def embed(i, b):
                add_half(b, tmp[:, b])
                if b == 0:
                    return
                for b in range(2):
                    t = i * 2 + b
                    dve.wait_ge(pg_sig, G.value + 1)
                    G.add()
                    step(dve.tensor_tensor(tmp[:, b], tmp[:, b], ple[:, t], ALU.mult))
                for b in range(2):
                    t = i * 2 + b
                    steps_done()
                    step(stt(res[:, t], res[:, t], ALPHA, tmp[:, b], ALU.mult, ALU.add))

            repeat(dve, DT // 2, two_tiles(embed, TURNS), *STD, (G, 2), (V, 4))
            steps_done()

            J = Count()
            step(dve.memset(u[:, :, 0:2], 0.0))
            steps_done()

            def conv(i, b):
                w = [par[:, bass.ds(i * 8 + (C_CONV + 4 * b + k), 1)] for k in range(4)]
                add_half(b, u[:, b, 2:S + 2])
                tile_done()
                dve.wait_ge(cv_free, J.value + 1)
                step(dve.tensor_scalar(cv[:, b], u[:, b, 2:S + 2], w[2], w[3], ALU.mult, ALU.add))
                steps_done()
                step(stt(cv[:, b], u[:, b, 1:S + 1], w[1], cv[:, b], ALU.mult, ALU.add))
                steps_done()
                stt(cv[:, b], u[:, b, 0:S], w[0], cv[:, b], ALU.mult, ALU.add).then_inc(cv_done, 1)
                if b == 1:
                    J.add()

            repeat(dve, FT, two_tiles(conv), *STD, (J, 1), (V, 4))


            def down(final):
                def body(i):
                    n_s = 2 * U_DOWN_TILE
                    for s in range(n_s):
                        if not (final and s + AHEAD >= n_s):
                            last = (s + AHEAD) % U_DOWN_TILE == U_DOWN_TILE - 1
                            split_lo(s, (DOWN_LAST if last else BLK) * P)
                        U.add()
                        if s % U_DOWN_TILE == U_DOWN_TILE - 1:
                            b = s // U_DOWN_TILE
                            t = i * 2 + b
                            add_half(b, tmp[:, b])
                            tile_done()
                            dve.tensor_tensor(res[:, t], res[:, t], tmp[:, b], ALU.add).then_inc(res_tile, 1)
                return body

            repeat(dve, DT // 2 - 1, down(False), (U, 2 * U_DOWN_TILE), (T, 2), (H, 2))
            down(True)(DT // 2 - 1)
            norm(1)
            for g in LN_DVE:
                scale(g, C_LN2G)
                for t in range(GRAN * g, GRAN * g + GRAN):
                    dve.tensor_scalar(res[:, t], res[:, t], par[:, C_LN2B + t:C_LN2B + t + 1], None, ALU.add
                                      ).then_inc(out_dve, 1)

        @block.gpsimd
        def _(pool):
            pool.sem_inc(row_added[0], 2)
            pool.sem_inc(row_added[1], 2)
            pool.wait_ge(bank_free, 2 + 12)
            with pool.Fori(0, HEADS // 2) as j:
                pool.wait_ge(idx_mm, j + 1)
                pool.tensor_copy(qi_st[:], feat[:, j + T_QIDX]).then_inc(qi_staged, 1)

            V, R = Count(), Count()
            pool.wait_ge(ke_in, 16)

            def step(ins):
                ins.then_inc(pool_step, 1)
                V.add()

            def steps_done():
                pool.wait_ge(pool_step, V.value)

            def rope(i):
                for s in range(4):
                    j = i * 4 + s
                    pool.wait_ge(rot_read, R.value + 1)
                    pool.tensor_tensor(tmp[:, s % 2], tmp[:, s % 2], ke[:, K_SIN:K_SIN + S], ALU.mult
                                       ).then_inc(rot_mul, 1)
                    pool.tensor_tensor(qp[:, j], qp[:, j], ke[:, K_COS:K_COS + S], ALU.mult
                                       ).then_inc(rot_mul, 1)
                    R.add()

            repeat(pool, U_UK // 4, rope, (R, 4))
            pool.wait_ge(rot_done, 2 + 8)
            pool.wait_ge(bank_free, 2 + N_FEAT + DT + 40)

            with pool.Fori(0, HEADS // 2) as i:
                for par_ in range(2):
                    pool.wait_ge(sc_b, i * 2 + (par_ + 1))
                    if par_ == 0:
                        pool.tensor_copy(qp_st[:], qp[:, i])
                    pool.tensor_copy(qa_st[:], qa[:, i * 2 + par_])
                    pool.tensor_copy(qn_st[:], qn[:, i * 2 + par_]).then_inc(q_staged, 1)
                    pool.wait_ge(pv_mm, i * 2 + (par_ + 1))
                    pool.wait_ge(bank_free, 2 + N_FEAT + DT + 40 + U_UV)
                    pool.tensor_copy(v_st[:], v_mla[:, :, bass.ds(i * (2 * HD) + par_ * HD, HD)]
                                     ).then_inc(v_staged, 1)

            for n, k in enumerate(range(BLK, DT, 2)):
                pool.wait_ge(o_hi, 3 * (BLK // 2) + n + 1)
                pool.tensor_tensor(ob_hl[:, k:k + 2, S:2 * S], qn[:, k:k + 2], ob_hl[:, k:k + 2, 0:S].bitcast(F32),
                                   ALU.subtract).then_inc(o_lo_pool, 1)

            pool.wait_ge(p_hi, 1)
            pool.tensor_tensor(p_hl[:, :, S:2 * S], p_raw[:], p_hl[:, :, 0:S].bitcast(F32), ALU.subtract
                               ).then_inc(p_lo, 1)

            A = Count()

            def add_row(w, t, b):
                for n, (done, new) in enumerate(((res_tile, res[:, t]), (sq_done, sq[:, b]))):
                    pool.wait_ge(row_added[n], A.value + 2)
                    pool.wait_ge(done, A.value + 1 + w)
                    pool.tensor_tensor(rows[:, n], rows[:, n], new, ALU.add).then_inc(row_added[n], 1)
                A.add()

            def add_rows(w):
                def body(i):
                    for b in range(2):
                        add_row(w, i * 2 + b, b)
                repeat(pool, DT // 2 - 1, body, (A, 2))
                add_row(w, DT - 2, 0)

            def clear_rows():
                step(pool.memset(rows[:], 0.0))
                steps_done()

            def norm(w):
                pool.wait_ge(sq_done, DT * (w + 1))
                pool.wait_ge(ln_mean, w + 1)
                for g in LN_POOL:
                    step(pool.tensor_tensor(chunk(g), chunk(g), over_tiles(mean), ALU.subtract))
                steps_done()
                pool.wait_ge(ln_rstd, w + 1)
                for g in LN_POOL:
                    ins = pool.tensor_tensor(chunk(g), chunk(g), over_tiles(rstd), ALU.mult)
                    if w == 0:
                        step(ins)
                        steps_done()
                        for t in range(GRAN * g, GRAN * g + GRAN):
                            ins = pool.tensor_scalar(res[:, t], res[:, t], par[:, C_LN1G + t:C_LN1G + t + 1],
                                                     par[:, C_LN1B + t:C_LN1B + t + 1], ALU.mult, ALU.add)
                    ins.then_inc(ln_pool, 1)

            pool.wait_ge(m_lo, DT)
            clear_rows()
            add_rows(0)
            norm(0)
            for g in LN_DVE:
                pool.wait_ge(x1_lo, g + 1)
                for t in range(GRAN * g, GRAN * g + GRAN):
                    step(pool.tensor_scalar(res[:, t], res[:, t], 1.0, par[:, C_LN1B + t:C_LN1B + t + 1],
                                            ALU.mult, ALU.add))
            steps_done()
            pool.sem_inc(x1_kept, 1)

            J = Count()
            pool.sem_inc(cv_free, 1)
            pool.sem_inc(act_lo, 1)

            def activate(j):
                pool.wait_ge(act_lo, J.value + 1)
                pool.wait_ge(sig_done, J.value + 1)
                step(pool.tensor_tensor(av[:], sig[:], cv[:, 0], ALU.mult))
                pool.wait_ge(cv_done, 2 * J.value + 2)
                steps_done()
                step(pool.tensor_tensor(av[:], av[:], cv[:, 1], ALU.mult))
                steps_done()
                pool.sem_inc(cv_free, 1)
                step(pool.tensor_copy(act_hl[:, j, 0:S], av[:]))
                steps_done()
                pool.tensor_tensor(act_hl[:, j, S:2 * S], av[:], act_hl[:, j, 0:S].bitcast(F32), ALU.subtract
                                   ).then_inc(act_lo, 1)
                J.add()

            repeat(pool, FT, activate, (J, 1), (V, 3))
            clear_rows()
            add_rows(1)
            norm(1)



def feature_tiles(w_in):
    at = np.cumsum([0, HEADS * HD, HD, HD, HEADS * ROPE, ROPE, HEADS, LORA, LORA, ROPE, 2 * D])
    q_a, k_a, v_a, q_idx, k_idx, w_idx, c_q, c_kv, k_pe, gates = (
        w_in[:, a:b] for a, b in zip(at[:-1], at[1:]))
    pad = np.zeros((D, ROPE - HEADS), w_in.dtype)
    first = np.concatenate([k_idx, k_pe, w_idx, pad, k_idx, k_a, v_a, q_idx, c_q, c_kv], axis=1)
    return first, q_a, gates


def units_two_per_tile(w):
    n = w.shape[1] // P
    return w.reshape(2, BLK, P, n, P).transpose(3, 0, 2, 1, 4).reshape(2 * n, P, UNIT)


def units_by_turns(w):
    u = units_two_per_tile(w)
    return u.reshape(-1, 2, 2, P, UNIT).transpose(0, 2, 1, 3, 4).reshape(u.shape)


def units_of_tiles(w, per):
    k, n = w.shape[0] // P, w.shape[1] // P
    return w.reshape(k, P, n // per, per, P).transpose(2, 1, 3, 0, 4).reshape(n // per, P, UNIT)


def in_pairs(a, b):
    k = a.shape[0]
    return np.stack([a.reshape(k, -1, P), b.reshape(k, -1, P)], axis=2).reshape(k, -1)


def by_tile(v):
    return v.reshape(-1, P).T


def feature_major(a):
    return np.ascontiguousarray(a.T.reshape(-1, P, S).transpose(1, 0, 2))


def constants():
    t = np.arange(S)
    diff = t[:, None] - t[None, :]
    sc = np.concatenate([diff[0:P, 0:P], diff[P:S, 0:S]], axis=1)
    masks = np.stack([np.where(sc >= 0, 0.0, NEG), sc]).astype(np.float32)
    inv = np.float32(10000.0) ** (-np.arange(0, ROPE, 2, dtype=np.float32) / np.float32(ROPE))
    ang = inv[:, None] * t.astype(np.float32)[None, :]
    cos, sin = (np.tile(f(ang).astype(np.float32), (4, 1)) for f in (np.cos, np.sin))
    rot = np.zeros((P, P), np.float32)
    for i in range(P):
        j, r = divmod(i, ROPE)
        if r < ROPE // 2:
            rot[j * ROPE + r + ROPE // 2, i] = -1.0
        else:
            rot[j * ROPE + r - ROPE // 2, i] = 1.0
    dup = np.zeros((P, P), np.float32)
    dup_rot = np.zeros((P, P), np.float32)
    for i in range(P):
        dup[ROPE + i % ROPE, i] = 1.0
        dup_rot[ROPE:, i] = rot[i // ROPE * ROPE:i // ROPE * ROPE + ROPE, i]
    stay = np.concatenate([np.eye(P, dtype=np.float32), np.full((P, P), 1.0 / D, np.float32)], axis=1)
    early = np.concatenate([cos, sin, rot, dup, dup_rot], axis=1)
    return masks, stay, early


def kernel(**inputs):
    import concourse.bacc as bacc
    from concourse.bass_utils import run_bass_kernel_spmd

    a = {k: np.asarray(v) for k, v in inputs.items()}
    w = {k: v[0] for k, v in a.items() if k != "x"}
    first, q_a, gates = feature_tiles(w["w_in"])
    w_uq = w["w_uq"]
    w_uq = np.concatenate([w_uq[:, :, HD:].reshape(LORA, -1), w_uq[:, :, :HD].reshape(LORA, -1)], axis=1)
    w_uv = w["w_uv"].reshape(LT, P, U_UV, S).transpose(2, 1, 0, 3).reshape(U_UV, P, UNIT)
    down = np.zeros((DT, P, U_DOWN_TILE * BLK, P), w["w_down"].dtype)
    down[:, :, 0:FT] = w["w_down"].reshape(FT, P, DT, P).transpose(2, 1, 0, 3)
    down = down.reshape(DT, P, U_DOWN_TILE, UNIT).transpose(0, 2, 1, 3).reshape(-1, P, UNIT)
    stream = np.concatenate([
        units_two_per_tile(first), units_two_per_tile(q_a),
        units_of_tiles(w_uq, 2), units_of_tiles(w["w_uk"].reshape(LORA, -1), 2), w_uv,
        units_two_per_tile(in_pairs(gates[:, :D], gates[:, D:])),
        units_by_turns(in_pairs(w["w_branch_a"], w["w_branch_b"])),
        units_by_turns(w["w_o"]), units_of_tiles(w["w_pe"], 4), units_by_turns(w["w_pg"]),
        units_two_per_tile(in_pairs(w["w_up"][:, :FF], w["w_up"][:, FF:])), down])
    assert stream.shape[0] == U_ALL

    conv = np.concatenate([w["conv_w"], w["conv_b"][None]])
    conv = conv.reshape(4, 2, FT, P).transpose(3, 2, 1, 0).reshape(P, -1)
    slopes = np.tile(-np.exp2(-8.0 * np.arange(1, HEADS + 1) / HEADS).astype(np.float32), (P, 1))
    eps = np.tile(np.array([LN_EPS, RMS_EPS, RMS_EPS / SCALE_B ** 2], np.float32), (P, 1))
    params = np.concatenate([conv, slopes] + [by_tile(w[n]) for n in (
        "ln1_g", "ln1_b", "ln2_g", "ln2_b", "b_pg", "q_a_norm", "kv_a_norm")] + [eps], axis=1)
    masks, stay, early = constants()
    arrays = {
        "stream": stream, "x_t": feature_major(a["x"][0]), "p_t": feature_major(w["p"][0]),
        "params": params, "consts_stay": stay, "consts_early": early, "masks": masks,
    }
    arrays = {k: np.ascontiguousarray(v) for k, v in arrays.items()}

    nc = bacc.Bacc("TRN2", target_bir_lowering=False, num_devices=1, dynamic_dma_scratch_size=1024)
    args = [nc.dram_tensor(k, v.shape, F32, kind="ExternalInput").ap() for k, v in arrays.items()]
    args.append(nc.dram_tensor("out", (P, DT, S), F32, kind="ExternalOutput").ap())
    hybrid_block(nc, *args)
    r = run_bass_kernel_spmd(nc, [arrays], core_ids=[0])
    y = np.asarray(r.results[0]["out"])
    return y.transpose(2, 1, 0).reshape(1, S, D)
```
